# Optimizing a Trainium2 kernel written in Bass

```python
import math
import jax, jax.numpy as jnp
from jax import lax
import numpy as np
import jax
import jax.numpy as jnp

D_MODEL = 1024
BATCH = 1
SEQ = 512
DEPTH = 1

N_HEADS = 8
HEAD_DIM = 64
V_DIM = 2 * HEAD_DIM
QK_WIDTH = N_HEADS * 2 * HEAD_DIM
ATTN_WIDTH = N_HEADS * V_DIM
LRU_WIDTH = D_MODEL
LRU_BLOCKS = 8
LRU_BLOCK = LRU_WIDTH // LRU_BLOCKS
CONV_WIDTH = 4
LRU_C = 8.0
D_FF = 4 * D_MODEL
N_BUCKETS = 32
MAX_DISTANCE = 128
Q_BLOCK = 128
EPS = 1e-6
IN_WIDTH = 3 * QK_WIDTH // 2 * 0 + QK_WIDTH + QK_WIDTH + ATTN_WIDTH + 2 * LRU_WIDTH + 2 * D_MODEL


def rmsnorm(x, g):
    x32 = x.astype(jnp.float32)
    y = x32 * lax.rsqrt(jnp.mean(jnp.square(x32), axis=-1, keepdims=True) + EPS)
    return (y * g.astype(jnp.float32)).astype(x.dtype)

def rel_bucket(n):
    max_exact = N_BUCKETS // 2
    n = jnp.maximum(n, 0)
    nf = jnp.maximum(n, 1).astype(jnp.float32)
    large = max_exact + (jnp.log(nf / max_exact) / math.log(MAX_DISTANCE / max_exact)
                         * (N_BUCKETS - max_exact)).astype(jnp.int32)
    large = jnp.minimum(large, N_BUCKETS - 1)
    return jnp.where(n < max_exact, n, large)

def diff_attention(q, k, v, q_g, k_g, rel_bias, lam, subln_g, lambda_init):
    B, S = q.shape[0], q.shape[1]
    q = rmsnorm(q, q_g)
    k = rmsnorm(k, k_g)
    nb = S // Q_BLOCK
    qb = jnp.transpose(q.reshape(B, nb, Q_BLOCK, N_HEADS, 2, HEAD_DIM), (1, 0, 2, 3, 4, 5))
    k_pos = jnp.arange(S, dtype=jnp.int32)
    scale = HEAD_DIM ** -0.5
    bias_tab = rel_bias.astype(jnp.float32)

    def one_block(args):
        q_blk, blk = args
        q_pos = blk * Q_BLOCK + jnp.arange(Q_BLOCK, dtype=jnp.int32)
        rel = q_pos[:, None] - k_pos[None, :]
        bias = jnp.transpose(bias_tab[rel_bucket(rel)], (2, 0, 1))
        logits = jnp.einsum('bqhcd,bkhcd->bhcqk', q_blk, k).astype(jnp.float32) * scale
        logits = logits + bias[None, :, None]
        logits = jnp.where(rel >= 0, logits, -jnp.inf)
        p = jax.nn.softmax(logits, axis=-1)
        attn = p[:, :, 0] - lam * p[:, :, 1]
        return jnp.einsum('bhqk,bkhe->bqhe', attn.astype(v.dtype), v)

    out = lax.map(one_block, (qb, jnp.arange(nb, dtype=jnp.int32)))
    out = jnp.transpose(out, (1, 0, 2, 3, 4)).reshape(B, S, N_HEADS, V_DIM)
    out = rmsnorm(out, subln_g) * (1.0 - lambda_init)
    return out.reshape(B, S, ATTN_WIDTH)

def rg_lru_branch(xr, gr, conv_w, conv_b, w_a, b_a, w_x, b_x, lru_lambda):
    B, S, W = xr.shape
    gate = jax.nn.gelu(gr)
    xpad = jnp.pad(xr, ((0, 0), (CONV_WIDTH - 1, 0), (0, 0)))
    xc = conv_b
    for tap in range(CONV_WIDTH):
        xc = xc + xpad[:, tap:tap + S] * conv_w[tap]
    xblk = xc.reshape(B, S, LRU_BLOCKS, LRU_BLOCK)
    r = jax.nn.sigmoid(jnp.einsum('bsne,nef->bsnf', xblk, w_a) + b_a).reshape(B, S, W)
    i = jax.nn.sigmoid(jnp.einsum('bsne,nef->bsnf', xblk, w_x) + b_x).reshape(B, S, W)
    log_a = -LRU_C * r.astype(jnp.float32) * jax.nn.softplus(-lru_lambda.astype(jnp.float32))
    a = jnp.exp(log_a)
    mult = jnp.sqrt(-jnp.expm1(2.0 * log_a))
    b = mult * (i * xc).astype(jnp.float32)

    def combine(c1, c2):
        a1, b1 = c1
        a2, b2 = c2
        return a1 * a2, a2 * b1 + b2

    _, h = lax.associative_scan(combine, (a, b), axis=1)
    return (h.astype(xr.dtype)) * gate

def first_inputs(seed: int = 0) -> dict:
    key = jax.random.key(seed)
    ks = jax.random.split(key, 24)
    f32 = jnp.float32
    nrm = lambda k, shape, scale: jax.random.normal(k, shape, f32) * scale
    gain = lambda k, shape: 1.0 + 0.05 * jax.random.normal(k, shape, f32)
    x = jax.random.normal(ks[0], (BATCH, SEQ, D_MODEL), f32)
    u = jax.random.uniform(ks[15], (DEPTH, LRU_WIDTH), f32, minval=0.9, maxval=0.999)
    a0 = u ** (1.0 / LRU_C)
    lru_lambda = jnp.log(a0) - jnp.log1p(-a0)
    return {
        'x': x,
        'norm_mix_g': gain(ks[1], (DEPTH, D_MODEL)),
        'w_in': nrm(ks[2], (DEPTH, D_MODEL, IN_WIDTH), D_MODEL ** -0.5),
        'q_norm_g': gain(ks[3], (DEPTH, HEAD_DIM)),
        'k_norm_g': gain(ks[4], (DEPTH, HEAD_DIM)),
        'lambda_q1': nrm(ks[5], (DEPTH, HEAD_DIM), 0.1),
        'lambda_k1': nrm(ks[6], (DEPTH, HEAD_DIM), 0.1),
        'lambda_q2': nrm(ks[7], (DEPTH, HEAD_DIM), 0.1),
        'lambda_k2': nrm(ks[8], (DEPTH, HEAD_DIM), 0.1),
        'subln_g': gain(ks[9], (DEPTH, V_DIM)),
        'conv_w': nrm(ks[10], (DEPTH, CONV_WIDTH, LRU_WIDTH), CONV_WIDTH ** -0.5),
        'conv_b': nrm(ks[11], (DEPTH, LRU_WIDTH), 0.02),
        'w_rg_a': nrm(ks[12], (DEPTH, LRU_BLOCKS, LRU_BLOCK, LRU_BLOCK), LRU_BLOCK ** -0.5),
        'b_rg_a': nrm(ks[13], (DEPTH, LRU_BLOCKS, LRU_BLOCK), 0.02),
        'w_rg_x': nrm(ks[14], (DEPTH, LRU_BLOCKS, LRU_BLOCK, LRU_BLOCK), LRU_BLOCK ** -0.5),
        'b_rg_x': nrm(ks[16], (DEPTH, LRU_BLOCKS, LRU_BLOCK), 0.02),
        'lru_lambda': lru_lambda,
        'w_proj_attn': nrm(ks[17], (DEPTH, ATTN_WIDTH, D_MODEL), ATTN_WIDTH ** -0.5),
        'w_proj_rnn': nrm(ks[18], (DEPTH, LRU_WIDTH, D_MODEL), LRU_WIDTH ** -0.5),
        'w_out': nrm(ks[19], (DEPTH, D_MODEL, D_MODEL), D_MODEL ** -0.5),
        'norm_mlp_g': gain(ks[20], (DEPTH, D_MODEL)),
        'w_up': nrm(ks[21], (DEPTH, D_MODEL, D_FF), D_MODEL ** -0.5),
        'w_down': nrm(ks[22], (DEPTH, D_FF, D_MODEL), D_FF ** -0.5),
        'rel_bias': nrm(ks[23], (N_BUCKETS, N_HEADS), 0.5),
    }

def first_block(x, norm_mix_g, w_in, q_norm_g, k_norm_g, lambda_q1, lambda_k1, lambda_q2, lambda_k2,
              subln_g, conv_w, conv_b, w_rg_a, b_rg_a, w_rg_x, b_rg_x, lru_lambda,
              w_proj_attn, w_proj_rnn, w_out, norm_mlp_g, w_up, w_down, rel_bias):
    B, S, _ = x.shape
    offs = np.cumsum([QK_WIDTH, QK_WIDTH, ATTN_WIDTH, LRU_WIDTH, LRU_WIDTH, D_MODEL]).tolist()
    for l in range(DEPTH):
        lambda_init = 0.8 - 0.6 * math.exp(-0.3 * l)
        h = rmsnorm(x, norm_mix_g[l])
        proj = jnp.einsum('bsd,de->bse', h, w_in[l])
        q, k, v, xr, gr, g_attn, g_rnn = jnp.split(proj, offs, axis=-1)
        q = q.reshape(B, S, N_HEADS, 2, HEAD_DIM)
        k = k.reshape(B, S, N_HEADS, 2, HEAD_DIM)
        v = v.reshape(B, S, N_HEADS, V_DIM)
        lam = (jnp.exp(jnp.sum(lambda_q1[l].astype(jnp.float32) * lambda_k1[l].astype(jnp.float32)))
               - jnp.exp(jnp.sum(lambda_q2[l].astype(jnp.float32) * lambda_k2[l].astype(jnp.float32)))
               + lambda_init)
        attn_out = diff_attention(q, k, v, q_norm_g[l], k_norm_g[l], rel_bias, lam, subln_g[l], lambda_init)
        rnn_out = rg_lru_branch(xr, gr, conv_w[l], conv_b[l], w_rg_a[l], b_rg_a[l],
                                w_rg_x[l], b_rg_x[l], lru_lambda[l])
        y_attn = jnp.einsum('bse,ed->bsd', attn_out, w_proj_attn[l])
        y_rnn = jnp.einsum('bse,ed->bsd', rnn_out, w_proj_rnn[l])
        merged = jax.nn.sigmoid(g_attn) * y_attn + jax.nn.sigmoid(g_rnn) * y_rnn
        x = x + jnp.einsum('bsd,de->bse', merged, w_out[l])
        h2 = rmsnorm(x, norm_mlp_g[l])
        up = jnp.square(jax.nn.relu(jnp.einsum('bsd,df->bsf', h2, w_up[l])))
        x = x + jnp.einsum('bsf,fd->bsd', up, w_down[l])
    return x


BRANCH_WIDTH = D_MODEL // 2
N_BRANCH = 3
CONV_WIDTH_2 = BRANCH_WIDTH
CONV_K = 3
FOX_HEADS = BRANCH_WIDTH // HEAD_DIM
SWA_HEADS = BRANCH_WIDTH // HEAD_DIM
SWA_KV_HEADS = 2
SWA_GROUP = SWA_HEADS // SWA_KV_HEADS
WINDOW = 128
BLOCK = 128
MAX_DISTANCE_2 = WINDOW
MEM_LEN = 256
X_HEADS = 4
X_HEAD_DIM = D_MODEL // X_HEADS
_FF_RAW = -(-8 * D_MODEL // 3)
D_FF_2 = -(-_FF_RAW // 256) * 256
IN_COLS = (3 * CONV_WIDTH_2 + 3 * FOX_HEADS * HEAD_DIM + FOX_HEADS
           + (SWA_HEADS + 2 * SWA_KV_HEADS) * HEAD_DIM + N_BRANCH * D_MODEL)
RMS_EPS = 1e-6
NEG_INF = -1e30


def rms_norm(x, g):
    xf = x.astype(jnp.float32)
    y = xf * lax.rsqrt(jnp.mean(xf * xf, axis=-1, keepdims=True) + RMS_EPS)
    return (y * g.astype(jnp.float32)).astype(x.dtype)

def split_proj(proj):
    sizes = ([CONV_WIDTH_2] * 3 + [FOX_HEADS * HEAD_DIM] * 3 + [FOX_HEADS]
             + [SWA_HEADS * HEAD_DIM, SWA_KV_HEADS * HEAD_DIM, SWA_KV_HEADS * HEAD_DIM]
             + [N_BRANCH * D_MODEL])
    parts, off = [], 0
    for s in sizes:
        parts.append(proj[..., off:off + s])
        off += s
    return parts

def short_conv_branch(gate_b, gate_c, u, conv_w):
    z = gate_c * u
    y = lax.conv_general_dilated(
        z, conv_w[:, None, :].astype(z.dtype), window_strides=(1,),
        padding=[(CONV_K - 1, 0)], dimension_numbers=('NWC', 'WIO', 'NWC'),
        feature_group_count=CONV_WIDTH_2)
    return gate_b * y

def fox_branch(q, k, v, f_logit, f_bias):
    b, s = q.shape[0], q.shape[1]
    nb = s // BLOCK
    q = q.reshape(b, s, FOX_HEADS, HEAD_DIM)
    k = k.reshape(b, s, FOX_HEADS, HEAD_DIM)
    v = v.reshape(b, s, FOX_HEADS, HEAD_DIM)
    log_f = jax.nn.log_sigmoid(f_logit.astype(jnp.float32) + f_bias.astype(jnp.float32))
    c = jnp.cumsum(log_f, axis=1)
    c_k = c.transpose(0, 2, 1)
    q_blocks = q.reshape(b, nb, BLOCK, FOX_HEADS, HEAD_DIM).transpose(1, 0, 2, 3, 4)
    c_blocks = c.reshape(b, nb, BLOCK, FOX_HEADS).transpose(1, 0, 2, 3)
    starts = jnp.arange(nb, dtype=jnp.int32) * BLOCK
    k_pos = jnp.arange(s, dtype=jnp.int32)
    scale = HEAD_DIM ** -0.5

    def one_block(args):
        qi, ci, start = args
        logits = jnp.einsum('bqhd,bkhd->bhqk', qi, k).astype(jnp.float32) * scale
        logits = logits + ci.transpose(0, 2, 1)[..., None] - c_k[:, :, None, :]
        q_pos = start + jnp.arange(BLOCK, dtype=jnp.int32)
        causal = k_pos[None, :] <= q_pos[:, None]
        logits = jnp.where(causal[None, None], logits, NEG_INF)
        p = jax.nn.softmax(logits, axis=-1)
        return jnp.einsum('bhqk,bkhd->bqhd', p.astype(v.dtype), v)

    out = lax.map(one_block, (q_blocks, c_blocks, starts))
    return out.transpose(1, 0, 2, 3, 4).reshape(b, s, FOX_HEADS * HEAD_DIM)

def t5_bucket(n):
    n = jnp.maximum(n, 0)
    max_exact = N_BUCKETS // 2
    large = max_exact + (
        jnp.log(jnp.maximum(n, 1).astype(jnp.float32) / max_exact)
        / math.log(MAX_DISTANCE_2 / max_exact) * (N_BUCKETS - max_exact)).astype(jnp.int32)
    large = jnp.minimum(large, N_BUCKETS - 1)
    return jnp.where(n < max_exact, n, large)

def swa_sink_branch(q, k, v, rel_bias, sink):
    b, s = q.shape[0], q.shape[1]
    nb = s // BLOCK
    qb = q.reshape(b, nb, BLOCK, SWA_KV_HEADS, SWA_GROUP, HEAD_DIM)
    kb = k.reshape(b, nb, BLOCK, SWA_KV_HEADS, HEAD_DIM)
    vb = v.reshape(b, nb, BLOCK, SWA_KV_HEADS, HEAD_DIM)

    def band(t):
        prev = jnp.concatenate([jnp.zeros_like(t[:, :1]), t[:, :-1]], axis=1)
        return jnp.concatenate([prev, t], axis=2)

    k_band, v_band = band(kb), band(vb)
    tq = jnp.arange(BLOCK, dtype=jnp.int32)
    sk = jnp.arange(2 * BLOCK, dtype=jnp.int32)
    dist = BLOCK + tq[:, None] - sk[None, :]
    in_window = (dist >= 0) & (dist < WINDOW)
    key_pos = jnp.arange(nb, dtype=jnp.int32)[:, None] * BLOCK - BLOCK + sk[None, :]
    mask = in_window[None] & (key_pos >= 0)[:, None, :]
    bias = rel_bias.astype(jnp.float32)[t5_bucket(dist)]
    bias = bias.reshape(BLOCK, 2 * BLOCK, SWA_KV_HEADS, SWA_GROUP).transpose(2, 3, 0, 1)
    logits = jnp.einsum('bnqkgd,bnskd->bnkgqs', qb, k_band).astype(jnp.float32) * HEAD_DIM ** -0.5
    logits = jnp.where(mask[None, :, None, None], logits + bias, NEG_INF)
    sink_l = sink.astype(jnp.float32).reshape(SWA_KV_HEADS, SWA_GROUP)[None, None, :, :, None]
    m = jnp.maximum(logits.max(axis=-1), sink_l)
    p = jnp.exp(logits - m[..., None])
    denom = p.sum(axis=-1) + jnp.exp(sink_l - m)
    p = p / denom[..., None]
    out = jnp.einsum('bnkgqs,bnskd->bnqkgd', p.astype(v.dtype), v_band)
    return out.reshape(b, s, SWA_HEADS * HEAD_DIM)

def cross_attention(xn, mem_n, w_q, w_kv, w_o):
    b, s = xn.shape[0], xn.shape[1]
    q = (xn @ w_q).reshape(b, s, X_HEADS, X_HEAD_DIM)
    kv = mem_n @ w_kv
    k = kv[..., :X_HEADS * X_HEAD_DIM].reshape(b, -1, X_HEADS, X_HEAD_DIM)
    v = kv[..., X_HEADS * X_HEAD_DIM:].reshape(b, -1, X_HEADS, X_HEAD_DIM)
    logits = jnp.einsum('bshd,bmhd->bhsm', q, k).astype(jnp.float32) * X_HEAD_DIM ** -0.5
    p = jax.nn.softmax(logits, axis=-1)
    o = jnp.einsum('bhsm,bmhd->bshd', p.astype(v.dtype), v).reshape(b, s, X_HEADS * X_HEAD_DIM)
    return o @ w_o

def swiglu(xn, w_gate, w_up, w_down):
    return (jax.nn.silu(xn @ w_gate) * (xn @ w_up)) @ w_down

def second_inputs(seed: int = 0) -> dict:
    key = jax.random.key(seed)
    ks = jax.random.split(key, 22)
    f32 = jnp.float32

    def nrm(k, shape, scale):
        return scale * jax.random.normal(k, shape, f32)

    def gain(k, shape):
        return 1.0 + 0.1 * jax.random.normal(k, shape, f32)

    return {
        "x": nrm(ks[0], (BATCH, SEQ, D_MODEL), 1.0),
        "mem": nrm(ks[1], (BATCH, MEM_LEN, D_MODEL), 1.0),
        "mix_norm_g": gain(ks[2], (DEPTH, D_MODEL)),
        "w_in": nrm(ks[3], (DEPTH, D_MODEL, IN_COLS), D_MODEL ** -0.5),
        "forget_bias": 4.0 + 0.5 * jax.random.normal(ks[4], (DEPTH, FOX_HEADS), f32),
        "conv_w": nrm(ks[5], (DEPTH, CONV_K, CONV_WIDTH_2), CONV_K ** -0.5),
        "sink": nrm(ks[6], (DEPTH, SWA_HEADS), 0.5),
        "w_branch": nrm(ks[7], (DEPTH, N_BRANCH, BRANCH_WIDTH, D_MODEL), BRANCH_WIDTH ** -0.5),
        "w_mix_out": nrm(ks[8], (DEPTH, D_MODEL, D_MODEL), D_MODEL ** -0.5),
        "rel_bias": nrm(ks[9], (N_BUCKETS, SWA_HEADS), 0.5),
        "xattn_norm_g": gain(ks[10], (DEPTH, D_MODEL)),
        "mem_norm_g": gain(ks[11], (DEPTH, D_MODEL)),
        "w_xq": nrm(ks[12], (DEPTH, D_MODEL, X_HEADS * X_HEAD_DIM), D_MODEL ** -0.5),
        "w_xkv": nrm(ks[13], (DEPTH, D_MODEL, 2 * X_HEADS * X_HEAD_DIM), D_MODEL ** -0.5),
        "w_xo": nrm(ks[14], (DEPTH, X_HEADS * X_HEAD_DIM, D_MODEL), (X_HEADS * X_HEAD_DIM) ** -0.5),
        "ffn_norm_g": gain(ks[15], (DEPTH, D_MODEL)),
        "w_ffn_gate": nrm(ks[16], (DEPTH, D_MODEL, D_FF_2), D_MODEL ** -0.5),
        "w_ffn_up": nrm(ks[17], (DEPTH, D_MODEL, D_FF_2), D_MODEL ** -0.5),
        "w_ffn_down": nrm(ks[18], (DEPTH, D_FF_2, D_MODEL), D_FF_2 ** -0.5),
        "final_norm_g": gain(ks[19], (D_MODEL,)),
    }

def second_block(x, mem, mix_norm_g, w_in, forget_bias, conv_w, sink, w_branch, w_mix_out,
              rel_bias, xattn_norm_g, mem_norm_g, w_xq, w_xkv, w_xo, ffn_norm_g,
              w_ffn_gate, w_ffn_up, w_ffn_down, final_norm_g):
    b, s = x.shape[0], x.shape[1]
    for l in range(DEPTH):
        h = rms_norm(x, mix_norm_g[l])
        (c_b, c_c, c_u, f_q, f_k, f_v, f_g, s_q, s_k, s_v, gate_logits) = split_proj(h @ w_in[l])
        y_conv = short_conv_branch(c_b, c_c, c_u, conv_w[l])
        y_fox = fox_branch(f_q, f_k, f_v, f_g, forget_bias[l])
        y_swa = swa_sink_branch(s_q, s_k, s_v, rel_bias, sink[l])
        gates = jax.nn.sigmoid(gate_logits.reshape(b, s, N_BRANCH, D_MODEL))
        merged = (gates[:, :, 0] * (y_conv @ w_branch[l, 0])
                  + gates[:, :, 1] * (y_fox @ w_branch[l, 1])
                  + gates[:, :, 2] * (y_swa @ w_branch[l, 2]))
        x = x + merged @ w_mix_out[l]
        x = x + cross_attention(rms_norm(x, xattn_norm_g[l]), rms_norm(mem, mem_norm_g[l]),
                                w_xq[l], w_xkv[l], w_xo[l])
        x = x + swiglu(rms_norm(x, ffn_norm_g[l]), w_ffn_gate[l], w_ffn_up[l], w_ffn_down[l])
    return rms_norm(x, final_norm_g)


def setup_inputs(seed=0):
    out = dict(first_inputs(seed))
    for name, value in second_inputs(seed + 1).items():
        if name != "x":
            out[name + "_2"] = value
    return out


def reference(
    x, norm_mix_g, w_in, q_norm_g, k_norm_g, lambda_q1, lambda_k1, lambda_q2, lambda_k2,
    subln_g, conv_w, conv_b, w_rg_a, b_rg_a, w_rg_x, b_rg_x, lru_lambda, w_proj_attn,
    w_proj_rnn, w_out, norm_mlp_g, w_up, w_down, rel_bias, mem_2, mix_norm_g_2, w_in_2,
    forget_bias_2, conv_w_2, sink_2, w_branch_2, w_mix_out_2, rel_bias_2, xattn_norm_g_2,
    mem_norm_g_2, w_xq_2, w_xkv_2, w_xo_2, ffn_norm_g_2, w_ffn_gate_2, w_ffn_up_2, w_ffn_down_2,
    final_norm_g_2,
):
    x = first_block(
        x, norm_mix_g, w_in, q_norm_g, k_norm_g, lambda_q1, lambda_k1, lambda_q2, lambda_k2,
        subln_g, conv_w, conv_b, w_rg_a, b_rg_a, w_rg_x, b_rg_x, lru_lambda, w_proj_attn,
        w_proj_rnn, w_out, norm_mlp_g, w_up, w_down, rel_bias,
    )
    return second_block(
        x, mem_2, mix_norm_g_2, w_in_2, forget_bias_2, conv_w_2, sink_2, w_branch_2,
        w_mix_out_2, rel_bias_2, xattn_norm_g_2, mem_norm_g_2, w_xq_2, w_xkv_2, w_xo_2,
        ffn_norm_g_2, w_ffn_gate_2, w_ffn_up_2, w_ffn_down_2, final_norm_g_2,
    )


_drawn_inputs = setup_inputs


def setup_inputs(seed=0):
    import zlib

    import numpy as np

    out = dict(_drawn_inputs(seed))
    spreads = {}
    factors = {'lambda_q1': 29.455,
     'lambda_k2': 2.918,
     'b_rg_a': 8.0,
     'b_rg_x': 8.0,
     'forget_bias_2': 31.384,
     'sink_2': 8.0,
     'rel_bias_2': 2.722,
     'xattn_norm_g_2': 8.0,
     'mem_norm_g_2': 5.62,
     'ffn_norm_g_2': 3.867}
    for name, (base, spread) in spreads.items():
        noise = np.random.default_rng([zlib.crc32(name.encode()), seed]).standard_normal(out[name].shape)
        drawn = base * np.exp(spread * noise) if base else spread * noise
        out[name] = jnp.asarray(drawn.astype(out[name].dtype))
    for name, factor in factors.items():
        out[name] = (out[name] * factor).astype(out[name].dtype)
    return out
```

```python
import math
from contextlib import ExitStack

import numpy as np

import concourse.bass as bass
from concourse import mybir

F32 = mybir.dt.float32
F32R = mybir.dt.float32r
ALU = mybir.AluOpType
ACT = mybir.ActivationFunctionType
AX = mybir.AxisListType

P = 128
S = 512
D = 1024
DC = D // P
NB = S // P
HEADS = 8
MEM = 256
FF1 = 4096
FF2 = 2816
BUCKETS = 32
EPS = 1e-6
MASKED = -1e30
LAMBDA_INIT = 0.8 - 0.6 * math.exp(-0.3 * 0)
BIAS1_W, BIAS2_W = 640, 384

ROWS_A = [("norm_mix_g", 8), ("conv_w", 32), ("conv_b", 8), ("b_rg_a", 8), ("b_rg_x", 8),
          ("lru_lambda", 8), ("norm_mlp_g", 8)]
ROWS_B = [("mix_norm_g_2", 8), ("conv_w_2", 12), ("xattn_norm_g_2", 8), ("mem_norm_g_2", 8),
          ("ffn_norm_g_2", 8), ("final_norm_g_2", 8), ("subln_g", 1)]

PHASES = [
    ("qkv", HEADS, [0, 1, 2], [8, 8, 8]),
    ("xr0", 1, [0], [8]),
    ("rnn", DC - 1, [1, 0, 2], [8, 8, 2]),
    ("rnn_last", 1, [1, 2], [8, 2]),
    ("merge1", DC, [0, 1, 2, 3], [8, 8, 8, 8]),
    ("out1", 2, [0, 1, 2, 3], [8] * 4),
    ("mlp", 4, [0, 1, 2, 3] * 4, [8] * 16),
    ("fgate", 1, [3], [8]),
    ("fox", 4, [0, 1, 2], [8] * 3),
    ("swa_first", 1, [0, 1, 2], [8, 8, 8]),
    ("swa", 3, [2, 3, 0, 1], [8] * 4),
    ("swa_last", 1, [3, 0, 1], [8] * 3),
    ("merge2", DC, [0, 1, 2, 3, 1], [8, 8, 8, 8, 4]),
    ("out2", 2, [0, 1, 2, 3], [8] * 4),
    ("cross", 4, [0, 1, 2, 3, 0, 1], [8] * 6),
    ("xout", 2, [0, 1, 2, 3], [8] * 4),
    ("ffn", 2, [0, 1, 2, 3] * 6, [8] * 24),
    ("ffn_tail", 1, [0, 1, 2, 3] * 5, [8] * 12 + [6] * 8),
]
SLOTS = 4
TWO_LOADS = {("rnn", 2), ("rnn_last", 1), ("swa_first", 0), ("swa", 0), ("merge2", 4)}
N_ROW_LOADS = len(ROWS_A) - 1 + len(ROWS_B) + 4


def bucket(n):
    half = BUCKETS // 2
    if n < half:
        return n
    big = half + int(np.log(np.float32(n) / np.float32(half)) / math.log(128 / half) * (BUCKETS - half))
    return min(big, BUCKETS - 1)


def bucket_rows():
    causal = np.zeros((BUCKETS + 1, BIAS1_W), np.float32)
    window = np.zeros((BUCKETS + 1, BIAS2_W), np.float32)
    for m in range(BIAS1_W):
        n = 511 - m
        causal[bucket(n) if n >= 0 else BUCKETS, m] = 1.0
    for m in range(BIAS2_W):
        n = 255 - m
        window[bucket(n) if 0 <= n < 128 else BUCKETS, m] = 1.0
    return causal, window


class Units:

    def __init__(self):
        self.base, self.at = {}, [1] * SLOTS
        self.load_base, self.load_at = {}, [0] * SLOTS
        self.slots, self.tiles, self.iters = {}, {}, {}
        for name, iters, slots, tiles in PHASES:
            self.base[name], self.load_base[name] = list(self.at), list(self.load_at)
            self.slots[name], self.tiles[name], self.iters[name] = slots, tiles, iters
            for j, s in enumerate(slots):
                self.at[s] += iters
                self.load_at[s] += iters * (1 + ((name, j) in TWO_LOADS))

    def use(self, name, it, j):
        slots = self.slots[name]
        s = slots[j]
        return s, it * slots.count(s) + self.base[name][s] + slots[:j + 1].count(s)


    def landed(self, name, it, j):
        s = self.slots[name][j]
        loads = [1 + ((name, i) in TWO_LOADS) if t == s else 0 for i, t in enumerate(self.slots[name])]
        return it * (16 * sum(loads)) + 16 * (self.load_base[name][s] + sum(loads[:j + 1]))


class Causal:

    def __init__(self, parts):
        self.jobs = [(part, j) for j in range(NB) for part in range(parts)]

    def first(self, i):
        return 0

    def offset(self, i):
        return P * i * (i + 1) // 2

    def queries(self, j):
        return list(range(j, NB))


class Window(Causal):

    def first(self, i):
        return max(0, i - 1)

    def offset(self, i):
        return P * (2 * i - 1) if i else 0

    def queries(self, j):
        return [j, j + 1] if j + 1 < NB else [j]


class Chain:

    def __init__(self, eng, sem):
        self.eng, self.sem, self.base, self.k = eng, sem, 0, 0

    def mark(self, ins):
        self.k += 1
        ins.then_inc(self.sem, 1)

    def wait(self):
        self.eng.wait_ge(self.sem, self.base + self.k)

    def link(self, ins):
        self.mark(ins)
        self.wait()

    def enter(self, it, per):
        self.before, self.per = self.base + self.k, per
        self.base, self.k = self.before + it * per, 0

    def leave(self, iters):
        assert self.k == self.per, f"a body has {self.k} links, not {self.per}"
        self.base, self.k = self.before + iters * self.per, 0


def program(nc, x, out, w, causal_rows, window_rows):
    units = Units()
    with ExitStack() as top:
        scopes = [top]

        def sb(name, shape, dt=F32):
            return scopes[-1].enter_context(nc.sbuf_tensor(name, shape, dt))

        def push():
            scopes.append(ExitStack())

        def pop():
            scopes.pop().close()

        class Sems(dict):

            def __missing__(self, name):
                self[name] = top.enter_context(nc.semaphore(name))
                return self[name]

        S_ = Sems()

        ONCE = {
            "vector_step": ["tab_masked", "gain_taken", "par_taken", "brow_rows", "decay_abs", "lam_dots", "lam_row", "lam_taken",
                            "values_cleared", "place_made", "forget_abs", "forget_one_plus", "forget_cum",
                            "forget_cum_lo"],
            "scalar_step": ["lam_exp", "decay_exp", "forget_exp", "forget_ln", "forget_cum_hi", "mem_std"],
            "tensor_step": ["gain_done", "par_done", "brow_done", "lam_done", "forget_placed", "mem_stat"],
            "pool_step": ["ident_clear", "ones_made", "above_clear", "ident_made", "above_made", "gate_clear"],
        }

        def once(event):
            for name, events in ONCE.items():
                if event in events:
                    return S_[name], 1 + events.index(event)
            raise KeyError(event)

        def norm_event(tag, kind, n):
            k = int(tag[1]) - 1
            return S_["norm_" + kind], k * {"acc": DC + 1, "stat": 1, "std": 1}.get(kind, DC) + n

        X = sb("X", [P, DC, S])
        HH, HL = sb("HH", [P, DC, S], F32R), sb("HL", [P, DC, S], F32R)
        RAW = sb("RAW", [P, SLOTS, DC, P])
        WH, WL = sb("WH", [P, SLOTS, DC, P], F32R), sb("WL", [P, SLOTS, DC, P], F32R)
        RSTD = sb("RSTD", [P, S])
        ident = sb("ident", [P, P])
        identr = sb("identr", [P, P], F32R)
        ones = sb("ones", [P, P])
        above = sb("above", [P, P])
        halves = sb("halves", [P, P])
        PARAM = sb("PARAM", [P, 160])
        small = sb("small", [P, 80])
        EPSC = sb("EPSC", [P, 1])
        IND = sb("IND", [P, HEADS])
        SIDE = sb("SIDE", [P, 2])
        SEXP = sb("SEXP", [P, 8])
        gate = sb("gate", [P, 2])
        SUM, NMAX, RS = sb("SUM", [P, 8]), sb("NMAX", [P, 8]), sb("RS", [P, 8])
        column, n = {}, 0
        for name, rows in ROWS_A:
            column[name] = n
            n += rows
        n = 96
        for name, rows in ROWS_B:
            column[name] = n
            n += rows
        column["q_norm_g"], column["k_norm_g"] = n, n + 1
        QG, KG, SUBG = n, n + 1, column["subln_g"]
        HBA, HBX, LAMC, SINK, NSINK, FBIAS, QG8, SUBL = 0, 8, 24, 32, 40, 48, 56, 57
        NZC, HZC = 64, 72

        def par(name, i):
            return PARAM[:, bass.ds(column[name] + i, 1)]

        psum = [top.enter_context(nc.psum_tensor(f"bank{i}", [P, S], F32)) for i in range(8)]
        STAT, OUTB = psum[4], psum[7]
        WORK = [psum[5], psum[6]]

        SQ1, ACC1, STD1 = sb("SQ1", [P, 2, S]), sb("ACC1", [P, S]), sb("STD1", [P, S])

        push()
        AO = sb("AOH", [P, DC, S], F32R), sb("AOL", [P, DC, S], F32R)
        push()
        XTOK = sb("XTOK", [P, NB, D])
        SQ0 = sb("SQ0", [P, 2, S])
        ACC0, STD0 = sb("ACC0", [P, S]), sb("STD0", [P, S])
        VROWS = sb("VROWS", [P, 2, P])
        ONEHOT = sb("ONEHOT", [BUCKETS + 1, BIAS1_W + BIAS2_W])
        TAB = sb("TAB", [BUCKETS + 1, 2, HEADS])
        BROWH = sb("BROWH", [HEADS, BIAS1_W + BIAS2_W], F32R)
        BROWL = sb("BROWL", [HEADS, BIAS1_W + BIAS2_W], F32R)
        LAM = sb("LAM", [1, 4, 64])
        LAMS = sb("LAMS", [1, 8])
        SROW = sb("SROW", [1, 16])
        LOGT = sb("LOGT", [P, 8, 8])
        pop()
        push()

        def attention_memory(tag, parts, cols):
            m = {}
            m["QN"] = sb(tag + "QN", [P, 2, S])
            if tag == "a":
                m["RQ"] = sb(tag + "RQ", [P, 3, S])
                m["SQ"] = sb(tag + "SQ", [P, 3, S])
            m["QH"], m["QL"] = sb(tag + "QH", [P, 2, S], F32R), sb(tag + "QL", [P, 2, S], F32R)
            m["VR"] = sb(tag + "VR", [P, S])
            m["VH"] = sb(tag + "VH", [P, parts, NB, P], F32R)
            m["VL"] = sb(tag + "VL", [P, parts, NB, P], F32R)
            m["PR"] = sb(tag + "PR", [P, 2, cols])
            m["TH"], m["TL"] = sb(tag + "TH", [P, 2, S], F32R), sb(tag + "TL", [P, 2, S], F32R)
            if tag == "a":
                m["OR"] = sb(tag + "OR", [P, S])
            return m

        M1 = attention_memory("a", 1, 1280)
        BIASH, BIASL = sb("BIASH", [P, S], F32R), sb("BIASL", [P, S], F32R)
        pop()
        RO = sb("ROH", [P, DC, S], F32R), sb("ROL", [P, DC, S], F32R)
        push()
        XR = sb("XR", [P, S + 3])
        XC = sb("XC", [P, S])
        XCH, XCL = sb("XCH", [P, S], F32R), sb("XCL", [P, S], F32R)
        RT, IT = sb("RT", [P, S]), sb("IT", [P, S])
        AT, TT, MT = sb("AT", [P, S]), sb("TT", [P, S]), sb("MT", [P, S])
        HS, GT, G2 = sb("HS", [P, S]), sb("GT", [P, S]), sb("G2", [P, S])
        pop()
        push()
        MG = sb("MG", [P, DC, S])
        GA = sb("GA", [P, 3, S])
        SG = sb("SG", [P, 3, S])
        pop()
        pop()
        push()
        UH, UL = sb("UH", [P, DC, S], F32R), sb("UL", [P, DC, S], F32R)
        TU, SU = sb("TU", [P, 2, S]), sb("SU", [P, 2, S])
        pop()

        push()
        YC = sb("YCH", [P, 4, S], F32R), sb("YCL", [P, 4, S], F32R)
        push()
        FG, FA, FE, FU = (sb(n, [HEADS, S]) for n in ("FG", "FA", "FE", "FU"))
        FLN, FT, FONE = (sb(n, [HEADS, S]) for n in ("FLN", "FT", "FONE"))
        FCH, FCL = sb("FCH", [HEADS, S], F32R), sb("FCL", [HEADS, S], F32R)
        PLACE0, PLACE = sb("PLACE0", [HEADS, 224]), sb("PLACE", [HEADS, 224], F32R)
        pop()
        YF = sb("YFH", [P, 4, S], F32R), sb("YFL", [P, 4, S], F32R)
        YS = sb("YSH", [P, 4, S], F32R), sb("YSL", [P, 4, S], F32R)
        push()
        M2 = attention_memory("f", 2, 1280)
        push()
        FLEFT = sb("FLEFT", [P, S], F32R)
        FRIGHT = sb("FRIGHT", [P, S])
        FROW = sb("FROW", [P, 2, S], F32R)
        ABOVER = sb("ABOVER", [P, P], F32R)
        pop()
        CB, CC, CV = SQ1[:, 0, :], SQ1[:, 1, :], ACC1[:]
        ZP = sb("ZP", [P, S + 2])
        BIAS2 = sb("BIAS2H", [P, 2, 2 * P], F32R), sb("BIAS2L", [P, 2, 2 * P], F32R)
        pop()
        MGC = sb("MGCH", [P, DC, S], F32R), sb("MGCL", [P, DC, S], F32R)
        GA2, SG2 = sb("GA2", [P, 3, S]), sb("SG2", [P, 3, S])
        MX = sb("MX", [P, 2, S])
        pop()
        push()
        MEMC = sb("MEMH", [P, DC, MEM], F32R), sb("MEML", [P, DC, MEM], F32R)
        RSTDM = sb("RSTDM", [P, MEM])
        push()
        MTOK = sb("MTOK", [P, MEM // P, D])
        SQM, ACCM, STDM = sb("SQM", [P, 2, MEM]), sb("ACCM", [P, MEM]), sb("STDM", [P, MEM])
        pop()
        XO = sb("XOH", [P, DC, S], F32R), sb("XOL", [P, DC, S], F32R)
        XQ, XK, XV = sb("XQ", [P, 2, S]), sb("XK", [P, 2, MEM]), sb("XV", [P, 2, MEM])
        XQC = sb("XQH", [P, 2, S], F32R), sb("XQL", [P, 2, S], F32R)
        XKC = sb("XKH", [P, 2, MEM], F32R), sb("XKL", [P, 2, MEM], F32R)
        XVC = sb("XVH", [P, 2, 2 * P], F32R), sb("XVL", [P, 2, 2 * P], F32R)
        XPR = sb("XPR", [P, NB, MEM])
        XTC = sb("XTH", [P, 2, S], F32R), sb("XTL", [P, 2, S], F32R)
        pop()
        push()
        FF = sb("FFH", [P, DC, S], F32R), sb("FFL", [P, DC, S], F32R)
        FGA, FUP = sb("FGA", [P, 2, S]), sb("FUP", [P, 2, S])
        YG = sb("YG", [P, 2, S])
        YTOK = sb("YTOK", [P, NB, D])
        pop()

        GAIN = {"n1": "norm_mix_g", "n2": "norm_mlp_g", "n3": "mix_norm_g_2", "n4": "xattn_norm_g_2",
                "n5": "ffn_norm_g_2", "n6": "final_norm_g_2"}
        ACC, STD, SQS = ({tag: first if tag == "n1" else later for tag in GAIN}
                         for first, later in ((ACC0, ACC1), (STD0, STD1), (SQ0, SQ1)))

        scr = [nc.dram_tensor(f"bias_rows_{k}", [HEADS, BIAS1_W + BIAS2_W], F32).ap() for k in "hl"]

        tiles1 = [nc.dram_tensor(f"bias_tiles1_{k}", [HEADS, P, S], F32).ap() for k in "hl"]
        tiles2 = [nc.dram_tensor(f"bias_tiles2_{k}", [HEADS, P, 2 * P], F32).ap() for k in "hl"]

        def toeplitz_rows(k, off, width):
            a = scr[k]
            return bass.AP(a.tensor, a.offset + off + P - 1, [[BIAS1_W + BIAS2_W, HEADS], [-1, P], [1, width]])

        def mem_after(e):
            return [] if e < 4 else [2 * e - 8, 2 * e - 7]

        KIND1, KIND_FOX, KIND_SWA = Causal(1), Causal(2), Window(2)
        block = top.enter_context(nc.Block())

        @block.sync
        def _(sp):
            def load(name, it, j, pieces):
                s, c = units.use(name, it, j)
                sp.wait_ge(S_[f"unit_cut{s}"], c - 1)
                for p0, pn, k0, src, c0 in pieces:
                    kn, cn = src.shape[1], src.shape[2]
                    sp.dma_start(RAW[p0:p0 + pn, s, k0:k0 + kn, c0:c0 + cn], src).then_inc(S_[f"landed{s}"], 16)

            def cols(wt, c, tiles=DC, row=0):
                a = wt[bass.ds(row, tiles * P), bass.ds(c, P)]
                return [(0, P, 0, a.rearrange("(k p) n -> p k n", p=P), 0)]

            name, r = ROWS_A[0]
            sp.dma_start(VROWS[0:r, 0, :], w[name].rearrange("(r c) -> r c", c=P)).then_inc(S_["gain_landed"], 16)
            for half in range(2):
                sp.dma_start(XTOK[:, :, half * S:(half + 1) * S],
                             x[:, half * S:(half + 1) * S].rearrange("(t p) d -> p t d", p=P)
                             ).then_inc(S_[f"x_landed{half}"], 16)
            n = 0
            for rows, side in ((ROWS_A, 0), (ROWS_B, 1)):
                at = 0
                for name, r in rows:
                    if name == ROWS_A[0][0]:
                        at = r
                        continue
                    sp.dma_start(VROWS[at:at + r, side, :], w[name].rearrange("(r c) -> r c", c=P)
                                 ).then_inc(S_["rows_landed"], 16)
                    at, n = at + r, n + 1
                if side:
                    for g in ("q_norm_g", "k_norm_g"):
                        for half in range(2):
                            sp.dma_start(VROWS[at:at + 1, 1, 64 * half:64 * half + 64],
                                         w[g].rearrange("(o c) -> o c", o=1)).then_inc(S_["rows_landed"], 16)
                            n += 1
                        at += 1
            assert n == N_ROW_LOADS
            for j in range(3):
                load("qkv", 0, j, cols(w["w_in"], D * j))
            sp.dma_start(ONEHOT[:, 0:BIAS1_W], causal_rows).then_inc(S_["tab_landed"], 16)
            sp.dma_start(ONEHOT[:, BIAS1_W:], window_rows).then_inc(S_["tab_landed"], 16)
            sp.dma_start(TAB[0:BUCKETS, 0, :], w["rel_bias"]).then_inc(S_["tab_landed"], 16)
            sp.dma_start(TAB[0:BUCKETS, 1, :], w["rel_bias_2"]).then_inc(S_["tab_landed"], 16)
            for k, name in enumerate(("lambda_q1", "lambda_k1", "lambda_q2", "lambda_k2")):
                sp.dma_start(LAM[:, k, :], w[name].rearrange("(o c) -> o c", o=1)).then_inc(S_["lam_landed"], 16)
            sp.dma_start(small[0:HEADS, FBIAS:FBIAS + 1], w["forget_bias_2"].rearrange("(p o) -> p o", o=1)
                         ).then_inc(S_["lam_landed"], 16)
            sp.dma_start(SROW[:, 0:8], w["sink_2"].rearrange("(o c) -> o c", o=1)).then_inc(S_["lam_landed"], 16)
            sp.wait_ge(*once("brow_rows"))
            sp.dma_start(scr[0], BROWH[:].bitcast(F32)).then_inc(S_["brow_stored"], 16)
            sp.dma_start(scr[1], BROWL[:].bitcast(F32)).then_inc(S_["brow_stored"], 16)
            sp.wait_ge(S_["brow_stored"], 32)
            for k in range(2):
                sp.dma_start(tiles1[k][0:2], toeplitz_rows(k, 0, S)[0:2]).then_inc(S_["tiles_stored"], 16)
            sp.wait_ge(S_["tiles_stored"], 32)
            for k, tile in enumerate((BIASH, BIASL)):
                sp.dma_start(tile[:].bitcast(F32), tiles1[k][0]).then_inc(S_["bias_landed"], 16)
            for k in range(2):
                sp.dma_start(tiles1[k][2:HEADS], toeplitz_rows(k, 0, S)[2:HEADS]).then_inc(S_["tiles_stored"], 16)
            with sp.Fori(1, HEADS) as h:
                for j in range(3):
                    load("qkv", h, j, cols(w["w_in"], h * P + D * j))
            for k in range(2):
                sp.dma_start(tiles2[k], toeplitz_rows(k, BIAS1_W, 2 * P)).then_inc(S_["tiles_stored"], 16)
            def load_gates(name, n, j):
                load(name, n if name == "rnn" else 0, j,
                     [(0, P, k, w[m][bass.ds(n * P, P), :].rearrange("(k p) n -> p k n", p=P), 0)
                      for k, m in enumerate(("w_rg_a", "w_rg_x"))])

            load("xr0", 0, 0, cols(w["w_in"], D * 3))
            with sp.Fori(0, DC - 1) as n:
                load("rnn", n, 0, cols(w["w_in"], n * P + D * 4))
                load("rnn", n, 1, cols(w["w_in"], n * P + (D * 3 + P)))
                load_gates("rnn", n, 2)
            load("rnn_last", 0, 0, cols(w["w_in"], D * 5 - P))
            load_gates("rnn_last", DC - 1, 1)
            with sp.Fori(0, DC) as e:
                load("merge1", e, 0, cols(w["w_proj_attn"], e * P))
                load("merge1", e, 1, cols(w["w_in"], e * P + D * 5))
                load("merge1", e, 2, cols(w["w_in"], e * P + D * 6))
                load("merge1", e, 3, cols(w["w_proj_rnn"], e * P))
            with sp.Fori(0, 2) as i:
                for j in range(4):
                    load("out1", i, j, cols(w["w_out"], i * 4 * P + j * P))
            with sp.Fori(0, 4) as g:
                for j in range(8):
                    load("mlp", g, j, cols(w["w_up"], g * D + j * P))
                for j in range(8):
                    load("mlp", g, 8 + j, cols(w["w_down"], j * P, row=g * D))
            C_FOX, C_FORGET, C_SWA, C_GATE = 3 * S, 6 * S, 6 * S + HEADS, 7 * S + HEADS + 2 * P
            load("fgate", 0, 0, cols(w["w_in_2"], C_FORGET))
            with sp.Fori(0, 4) as h:
                for j in range(3):
                    load("fox", h, j, cols(w["w_in_2"], h * P + (C_FOX + S * j)))
            def swa_q(h):
                return [(0, P, 0, w["w_in_2"][:, bass.ds(h * 64 + (C_SWA + 256 * k), 64)]
                         .rearrange("(k p) n -> p k n", p=P), 64 * k) for k in range(2)]

            load("swa_first", 0, 0, swa_q(0))
            for j in range(2):
                load("swa_first", 0, 1 + j, cols(w["w_in_2"], C_SWA + S + P * j))
            with sp.Fori(0, 3) as h:
                load("swa", h, 0, [(0, P, 0, w["w_in_2"][:, bass.ds(h * 64 + (C_SWA + 64 + 256 * k), 64)]
                                    .rearrange("(k p) n -> p k n", p=P), 64 * k) for k in range(2)])
                for j in range(3):
                    load("swa", h, 1 + j, cols(w["w_in_2"], h * P + S * j))
            for j in range(3):
                load("swa_last", 0, j, cols(w["w_in_2"], 3 * P + S * j))
            wb = w["w_branch_2"]
            with sp.Fori(0, DC) as e:
                load("merge2", e, 0, cols(wb, e * P))
                for j in range(3):
                    load("merge2", e, 1 + j, cols(w["w_in_2"], e * P + (C_GATE + D * j)))
                load("merge2", e, 4, [(64 * k, 64, 0, wb[D + 256 * k:D + 256 * k + 256, bass.ds(e * P, P)]
                                       .rearrange("(k p) n -> p k n", p=64), 0) for k in range(2)])
            for i in range(2):
                for j in range(4):
                    load("out2", i, j, cols(w["w_mix_out_2"], i * 4 * P + j * P))
                if i == 0:
                    sp.wait_ge(S_["mgc_lo"], DC)
                    sp.dma_start(MTOK[:], w["mem_2"].rearrange("(t p) d -> p t d", p=P)
                                 ).then_inc(S_["mem_landed"], 16)
            with sp.Fori(0, 4) as h:
                for j in range(2):
                    load("cross", h, j, cols(w["w_xq_2"], h * 2 * P + P * j))
                for j in range(4):
                    load("cross", h, 2 + j, cols(w["w_xkv_2"], h * 2 * P + (D * (j // 2) + P * (j % 2))))
            for i in range(2):
                for j in range(4):
                    load("xout", i, j, cols(w["w_xo_2"], i * 4 * P + j * P))
            with sp.Fori(0, 2) as g:
                for j in range(8):
                    load("ffn", g, 2 * j, cols(w["w_ffn_gate_2"], g * D + j * P))
                    load("ffn", g, 2 * j + 1, cols(w["w_ffn_up_2"], g * D + j * P))
                for j in range(8):
                    load("ffn", g, 16 + j, cols(w["w_ffn_down_2"], j * P, row=g * D))
            for j in range(6):
                load("ffn_tail", 0, 2 * j, cols(w["w_ffn_gate_2"], 2 * D + j * P))
                load("ffn_tail", 0, 2 * j + 1, cols(w["w_ffn_up_2"], 2 * D + j * P))
            for j in range(8):
                load("ffn_tail", 0, 12 + j, cols(w["w_ffn_down_2"], j * P, tiles=6, row=2 * D))
            for t in range(NB):
                sp.wait_ge(S_["y_scaled_v" if t % 2 == 0 else "y_scaled_a"], t // 2 + 1)
                sp.dma_start(out[t * P:(t + 1) * P, :], YTOK[:, t, :]).then_inc(S_["out_stored"], 16)
            sp.wait_ge(S_["out_stored"], 16 * NB)

        @block.gpsimd
        def _(pool):
            nc.gpsimd.memset(ident[:], 0.0).then_inc(once("ident_clear")[0], 1)
            nc.gpsimd.memset(ones[:], 1.0).then_inc(once("ones_made")[0], 1)
            nc.gpsimd.memset(above[:], 0.0).then_inc(once("above_clear")[0], 1)
            pool.wait_ge(*once("ident_clear"))
            nc.gpsimd.affine_select(out=ident[:], in_=ident[:], compare_op=ALU.not_equal, fill=1.0, base=0,
                                    pattern=[[-1, P]], channel_multiplier=1).then_inc(once("ident_made")[0], 1)

            pool.wait_ge(*once("above_clear"))
            nc.gpsimd.affine_select(out=above[:], in_=above[:], compare_op=ALU.is_ge, fill=MASKED, base=0,
                                    pattern=[[-1, P]], channel_multiplier=1).then_inc(once("above_made")[0], 1)

            for s in range(SLOTS):
                pool.sem_inc(S_[f"unit_cut{s}"], 1)
                pool.sem_inc(S_[f"hi_made{s}"], 1)
            nc.gpsimd.memset(gate[:], 0.0).then_inc(once("gate_clear")[0], 1)
            pool.wait_ge(*once("gate_clear"))

            def cut(name, it, j):
                s, c = units.use(name, it, j)
                k = units.tiles[name][j]
                pool.wait_ge(S_[f"landed{s}"], units.landed(name, it, j))
                pool.wait_ge(S_[f"product{s}"], c - 1)
                nc.gpsimd.tensor_tensor(gate[:, 1:2], gate[:, 0:1], gate[:, 0:1], ALU.add)
                nc.gpsimd.tensor_scalar(WH[:, s, 0:k, :], RAW[:, s, 0:k, :], 1.0, 1.0, ALU.mult, ALU.mult
                                        ).then_inc(S_[f"hi_made{s}"], 1)
                pool.wait_ge(S_[f"hi_made{s}"], c)
                nc.gpsimd.tensor_tensor(WL[:, s, 0:k, :], RAW[:, s, 0:k, :], WH[:, s, 0:k, :].bitcast(F32),
                                        ALU.subtract).then_inc(S_[f"unit_cut{s}"], 1)

            for name, iters, slots, _t in PHASES:
                if iters == 1:
                    for j in range(len(slots)):
                        cut(name, 0, j)
                else:
                    with pool.Fori(0, iters) as it:
                        for j in range(len(slots)):
                            cut(name, it, j)


        @block.tensor
        def _(pe):
            mm = nc.tensor.matmul

            for s in range(SLOTS):
                pe.sem_inc(S_[f"product{s}"], 1)

            def product(name, it, j, hi, lo, n=S, ready=None):
                s, c = units.use(name, it, j)
                tiles = units.tiles[name][j]
                pe.wait_ge(S_[f"unit_cut{s}"], c)
                pe.wait_ge(S_[f"taken{s}"], c - 1)
                for k in range(tiles):
                    if ready:
                        ready(k)
                    mm(psum[s][:, 0:n], WH[:, s, k, :], hi(k), start=(k == 0), stop=False)
                    yield
                    mm(psum[s][:, 0:n], WH[:, s, k, :], lo(k), start=False, stop=False)
                    yield
                    last = mm(psum[s][:, 0:n], WL[:, s, k, :], hi(k), start=False, stop=(k == tiles - 1))
                    if k == tiles - 1:
                        last.then_inc(S_[f"product{s}"], 1)
                    yield

            def run(steps, n=10 ** 9):
                for _i in range(n):
                    if next(steps, "end") == "end":
                        return

            def chain(*gens):
                for g in gens:
                    yield from g

            def from_h(name, it, j, ready=None):
                return product(name, it, j, lambda k: HH[:, k, :], lambda k: HL[:, k, :], ready=ready)

            def cut_of(tag):
                def ready(k):
                    pe.wait_ge(*norm_event(tag, "hh", k + 1))
                    pe.wait_ge(*norm_event(tag, "hl", k + 1))
                return ready

            def norm_stat(tag, before=None):
                if before:
                    pe.wait_ge(*norm_event(before, "std", 1))
                pe.wait_ge(*norm_event(tag, "acc", DC + 1))
                mm(STAT[:], ones[:], ACC[tag][:], start=True, stop=True).then_inc(norm_event(tag, "stat", 0)[0], 1)

            pe.wait_ge(*once("ident_made"))
            for e in range(DC):
                if e % 4 == 0:
                    pe.wait_ge(S_[f"x_landed{e // 4}"], 16)
                if e >= 2:
                    pe.wait_ge(S_["n1_x"], e - 1)
                for t in range(NB):
                    last = nc.tensor.transpose(WORK[e % 2][:, t * P:(t + 1) * P], XTOK[:, t, e * P:(e + 1) * P],
                                               ident[:])
                last.then_inc(S_["xt_done"], 1)
                if e == 1:
                    pe.wait_ge(S_["gain_landed"], 16)
                    nc.tensor.transpose(OUTB[:, 0:8], VROWS[0:8, 0, :], ident[0:8, 0:8]
                                        ).then_inc(once("gain_done")[0], 1)
            pe.wait_ge(S_["rows_landed"], 16 * N_ROW_LOADS)
            pe.wait_ge(*once("gain_taken"))
            na, nb = sum(r for _, r in ROWS_A), sum(r for _, r in ROWS_B) + 2
            nc.tensor.transpose(OUTB[:, 0:na], VROWS[0:na, 0, :], ident[0:na, 0:na])
            nc.tensor.transpose(OUTB[:, 96:96 + nb], VROWS[0:nb, 1, :], ident[0:nb, 0:nb]
                                ).then_inc(once("par_done")[0], 1)
            pe.wait_ge(S_["tab_landed"], 64)
            pe.wait_ge(*once("tab_masked"))
            mm(psum[3][0:8, :], TAB[:, 0, :], ONEHOT[:, 0:512], start=True, stop=True)
            mm(psum[2][0:8, 0:128], TAB[:, 0, :], ONEHOT[:, 512:640], start=True, stop=True)
            mm(psum[2][0:8, 128:512], TAB[:, 1, :], ONEHOT[:, 640:1024], start=True, stop=True
               ).then_inc(once("brow_done")[0], 1)

            def stat(tag, n, lhs, rhs):
                if not isinstance(n, int) or n:
                    pe.wait_ge(S_[tag + "_stat_read"], n)
                mm(STAT[:], lhs, rhs, start=True, stop=True).then_inc(S_[tag + "_stat"], 1)

            def v_transpose(tag, M, h):
                s, c = units.use({"a": "qkv", "f": "fox"}[tag], h, 2)
                pe.wait_ge(S_[f"taken{s}"], c)
                pe.wait_ge(S_[tag + "_out_taken"], h + 1)
                for j in range(NB):
                    last = nc.tensor.transpose(OUTB[:, j * P:(j + 1) * P], M["VR"][:, j * P:(j + 1) * P], ident[:])
                last.then_inc(S_[tag + "_vt"], 1)

            def transpose_probs(tag, M, kind, h, n):
                part, j = kind.jobs[n]
                blocks = kind.queries(j)
                if n >= 2:
                    pe.wait_ge(S_[tag + "_pt_lo"], h * len(kind.jobs) + n)
                pe.wait_ge(S_[tag + "_probs"], h * NB + blocks[-1] + 1)
                for b, i in enumerate(blocks):
                    at = kind.offset(i) + (j - kind.first(i)) * P
                    last = nc.tensor.transpose(WORK[n % 2][:, b * P:(b + 1) * P], M["PR"][:, part, at:at + P],
                                               ident[:])
                last.then_inc(S_[tag + "_pt"], 1)

            def values(tag, M, kind, h, n):
                part, j = kind.jobs[n]
                J, blocks = len(kind.jobs), kind.queries(j)
                q0, wide = blocks[0] * P, len(blocks) * P
                pe.wait_ge(S_[tag + "_pt_hi"], h * J + n + 1)
                pe.wait_ge(S_[tag + "_pt_lo"], h * J + n + 2)
                for v, p in (("VH", "TH"), ("VH", "TL"), ("VL", "TH")):
                    last = mm(OUTB[:, q0:q0 + wide], M[v][:, part, j, :], M[p][:, n % 2, 0:wide],
                              start=(n == 0 and v == "VH" and p == "TH"), stop=(n == J - 1 and v == "VL"),
                              skip_group_check=True)
                if n == J - 1:
                    last.then_inc(S_[tag + "_pv"], 1)

            def attend(tag, M, kind, h, steps, share, add_bias, k_of=lambda part, k0, k1: None, stats=None):
                J = len(kind.jobs)
                pe.wait_ge(S_[tag + "_qk_hi"], h + 6 if kind is KIND_SWA else 2 * h + 2)
                pe.wait_ge(S_[tag + "_qk_lo"], h + 6 if kind is KIND_SWA else 2 * h + 2)
                for t in range(8):
                    part, i = t % 2, t // 2
                    if t < 2:
                        pe.wait_ge(S_[tag + "_pt_lo"], h * J + 1)
                    else:
                        pe.wait_ge(S_[tag + "_exp"], h * 8 + t - 1)
                    k0, k1 = kind.first(i) * P, (i + 1) * P
                    bank = WORK[t % 2][:, 0:k1 - k0]
                    rows = slice(64 * part, 64 * part + 64)
                    for q, k in (("QH", "QH"), ("QH", "QL"), ("QL", "QH")):
                        mm(bank, M[q][rows, 0, i * P:(i + 1) * P], M[k][rows, 1, k0:k1],
                           start=(q == "QH" and k == "QH"), stop=False, skip_group_check=True)
                    add_bias(h, t, part, i, bank, k0, k1).then_inc(S_[tag + "_score"], 1)
                    run(steps, share[0])
                    if t == 0 and kind is not KIND_SWA:
                        v_transpose(tag, M, h)
                run(steps, share[1])
                pe.wait_ge(S_[tag + "_exp"], h * 8 + 8)
                transpose_probs(tag, M, kind, h, 0)
                transpose_probs(tag, M, kind, h, 1)
                if stats:
                    stats(0)
                v_cut = {KIND1: h + 1, KIND_FOX: 2 * h + 2, KIND_SWA: 10}[kind]
                pe.wait_ge(S_[tag + "_v_hi"], v_cut)
                pe.wait_ge(S_[tag + "_v_lo"], v_cut)
                if kind is KIND_SWA:
                    pe.wait_ge(S_[tag + "_out_taken"], h + 1)
                run(steps, share[2])
                if stats:
                    stats(1)
                for n in range(J):
                    run(steps, share[3])
                    values(tag, M, kind, h, n)
                    if n + 2 < J:
                        transpose_probs(tag, M, kind, h, n + 2)
                run(steps)

            def toeplitz(h, t, part, i, bank, k0, k1):
                if t == 0:
                    pe.wait_ge(S_["bias_landed"], 32 * h + 32)
                off = P * (NB - 1 - i)
                mm(bank, identr[:], BIASH[:, off:S], start=False, stop=False, skip_group_check=True)
                return mm(bank, identr[:], BIASL[:, off:S], start=False, stop=True, skip_group_check=True)

            def qk_stat1(h, n, side):
                pe.wait_ge(S_["a_qk_sq"], 2 * h + 1 + side)
                stat("a", n + side, halves[:], M1["SQ"][:, side, :])

            run(from_h("qkv", 0, 0, cut_of("n1")))
            norm_stat("n1")
            run(from_h("qkv", 0, 1))
            pe.wait_ge(*once("brow_rows"))
            pe.wait_ge(*norm_event("n1", "std", 1))
            values0 = from_h("qkv", 0, 2)
            for side in range(2):
                run(values0, 9)
                qk_stat1(0, 0, side)
            run(values0)
            pe.wait_ge(*once("lam_row"))
            pe.wait_ge(S_["lam_landed"], 96)
            mm(psum[3][:, 0:16], ones[0:1, :], SROW[0:1, 0:16], start=True, stop=True).then_inc(once("lam_done")[0], 1)

            def head1(h, last):
                steps = chain(from_h("xr0", 0, 0), from_h("rnn", 0, 0)) if last else \
                    chain(*[from_h("qkv", h + 1, j) for j in range(3)])
                attend("a", M1, KIND1, h, steps, (2, 8, 8, 3) if last else (5, 10, 10, 2), toeplitz,
                       stats=None if last else lambda side: qk_stat1(h + 1, 3 * h + 2, side))
                pe.wait_ge(S_["a_o_sq"], h + 1)
                stat("a", 3 * h + (2 if last else 4), ones[:], M1["SQ"][:, 2, :])

            with pe.Fori(0, HEADS - 1) as h:
                head1(h, False)
            head1(HEADS - 1, True)

            pe.wait_ge(S_["a_pt_lo"], HEADS * 4 + 1)
            def rnn_gates(n, name="rnn", it=None, j=2):
                s, c = units.use(name, n if it is None else it, j)
                pe.wait_ge(S_[f"unit_cut{s}"], c)
                pe.wait_ge(S_[f"taken{s}"], c - 1)
                pe.wait_ge(S_["gate_i_taken"], n + 1)
                pe.wait_ge(S_["xc_hi"], n + 1)
                pe.wait_ge(S_["xc_lo"], n + 1)
                for k, bank in enumerate((psum[s], WORK[0])):
                    mm(bank[:], WH[:, s, k, :], XCH[:], start=True, stop=False)
                    mm(bank[:], WH[:, s, k, :], XCL[:], start=False, stop=False)
                    last = mm(bank[:], WL[:, s, k, :], XCH[:], start=False, stop=True)
                last.then_inc(S_[f"product{s}"], 1)

            run(from_h("rnn", 0, 1))
            rnn_gates(0)
            with pe.Fori(1, DC - 1) as n:
                for j in range(2):
                    run(from_h("rnn", n, j))
                rnn_gates(n)
            run(from_h("rnn_last", 0, 0))
            rnn_gates(DC - 1, "rnn_last", 0, 1)

            def from_pair(name, it, j, pair, ready=None):
                return product(name, it, j, lambda k: pair[0][:, k, :], lambda k: pair[1][:, k, :], ready=ready)

            with pe.Fori(0, DC) as e:
                pe.wait_ge(S_["a_o_hi"], HEADS)
                pe.wait_ge(S_["a_o_lo"], HEADS)
                run(from_pair("merge1", e, 0, AO))
                run(from_h("merge1", e, 1))
                run(from_h("merge1", e, 2))
                pe.wait_ge(S_["ro_hi"], DC)
                pe.wait_ge(S_["ro_lo"], DC)
                run(from_pair("merge1", e, 3, RO))

            def cut_pair(hi, lo, base=0):
                def ready(k):
                    pe.wait_ge(S_[hi], base + k + 1)
                    pe.wait_ge(S_[lo], base + k + 1)
                return ready

            for i in range(2):
                for j in range(4):
                    run(from_pair("out1", i, j, AO, cut_pair("mg_hi", "mg_lo") if i == j == 0 else None))

            def mlp_group(g, first=False):
                for j in range(8):
                    run(from_h("mlp", g, j, cut_of("n2") if first and j == 0 else None))
                    if first and j == 0:
                        norm_stat("n2")
                for j in range(8):
                    run(from_pair("mlp", g, 8 + j, (UH, UL), cut_pair("u_hi", "u_lo", 8 * g) if j == 0 else None))

            mlp_group(0, True)
            with pe.Fori(1, 3) as g:
                mlp_group(g)
            mlp_group(3)

            run(from_h("fgate", 0, 0, cut_of("n3")))
            norm_stat("n3", "n2")
            for j in range(3):
                run(from_h("fox", 0, j))
            pe.wait_ge(*once("place_made"))
            pe.wait_ge(*once("forget_cum_hi"))
            pe.wait_ge(*once("forget_cum_lo"))
            for bank, (at_hi, at_lo) in ((0, (96, 64)), (1, (32, 0))):
                mm(WORK[bank][:], PLACE[:, at_hi:at_hi + P], FCH[:], start=True, stop=False)
                last = mm(WORK[bank][:], PLACE[:, at_lo:at_lo + P], FCL[:], start=False, stop=True)
            last.then_inc(once("forget_placed")[0], 1)

            def decay(h, t, part, i, bank, k0, k1):
                if t < 2:
                    pe.wait_ge(S_["f_row"], 2 * h + t + 1)
                mm(bank, FLEFT[:, i * P:(i + 1) * P], FROW[:, part, k0:k1], start=False, stop=False,
                   skip_group_check=True)
                return mm(WORK[t % 2][:, i * P:(i + 1) * P], identr[:], ABOVER[:], start=False, stop=True,
                          skip_group_check=True)

            def fox(h, steps):
                attend("f", M2, KIND_FOX, h, steps, (5, 12, 9, 1), decay)

            with pe.Fori(0, 3) as h:
                fox(h, chain(*[from_h("fox", h + 1, j) for j in range(3)]))
            fox(3, chain(from_h("swa_first", 0, 0), from_h("swa_first", 0, 1), from_h("swa_first", 0, 2)))

            s, c = units.use("swa_first", 0, 2)
            pe.wait_ge(S_[f"taken{s}"], c)
            pe.wait_ge(S_["f_out_taken"], 5)
            for j in range(NB):
                last = nc.tensor.transpose(OUTB[:, j * P:(j + 1) * P], M2["VR"][:, j * P:(j + 1) * P], ident[:])
            last.then_inc(S_["f_vt"], 1)

            def toeplitz2(h, t, part, i, bank, k0, k1):
                if t == 0:
                    pe.wait_ge(S_["bias2_landed"], 64 * h - 192)
                off = P if i == 0 else 0
                mm(bank, identr[:], BIAS2[0][:, part, off:], start=False, stop=False, skip_group_check=True)
                return mm(bank, identr[:], BIAS2[1][:, part, off:], start=False, stop=True, skip_group_check=True)

            with pe.Fori(0, 3) as h:
                attend("f", M2, KIND_SWA, h + 4, chain(*[from_h("swa", h, j) for j in range(4)]), (9, 12, 8, 1),
                       toeplitz2)
            attend("f", M2, KIND_SWA, 7, chain(*[from_h("swa_last", 0, j) for j in range(3)]), (7, 8, 4, 1),
                   toeplitz2)

            pe.wait_ge(S_["f_pt_lo"], 8 * 8 + 1)
            pe.wait_ge(S_["yc_lo"], 4)
            pe.wait_ge(S_["f_out_taken"], 9)
            with pe.Fori(0, DC) as e:
                s, c = units.use("merge2", e, 0)
                pe.wait_ge(S_[f"unit_cut{s}"], c)
                pe.wait_ge(S_[f"taken{s}"], c - 1)
                pe.wait_ge(S_["m2_fox_taken"], e + 1)
                for k in range(8):
                    bank, y = (psum[s], YC) if k < 4 else (WORK[0], YF)
                    mm(bank[:], WH[:, s, k, :], y[0][:, k % 4, :], start=(k % 4 == 0), stop=False)
                    mm(bank[:], WH[:, s, k, :], y[1][:, k % 4, :], start=False, stop=False)
                    last = mm(bank[:], WL[:, s, k, :], y[0][:, k % 4, :], start=False, stop=(k % 4 == 3))
                last.then_inc(S_[f"product{s}"], 1)
                for j in range(3):
                    run(from_h("merge2", e, 1 + j))
                run(from_pair("merge2", e, 4, YS))

            for e in range(DC):
                run(from_pair("out2", e // 4, e % 4, MGC, cut_pair("mgc_hi", "mgc_lo") if e == 0 else None))
                if e == 4:
                    pe.wait_ge(S_["mem_landed"], 16)
                for m in mem_after(e):
                    if m >= 2:
                        pe.wait_ge(S_["mem_lo"], m - 1)
                        pe.wait_ge(S_["mem_sq"], m - 1)
                    for t in range(MEM // P):
                        last = nc.tensor.transpose(WORK[m % 2][:, t * P:(t + 1) * P],
                                                   MTOK[:, t, m * P:(m + 1) * P], ident[:])
                    last.then_inc(S_["mem_t"], 1)
            run(from_h("cross", 0, 0, cut_of("n4")))
            norm_stat("n4", "n3")
            pe.wait_ge(S_["mem_acc"], DC + 1)
            mm(OUTB[:, 0:MEM], ones[:], ACCM[:], start=True, stop=True).then_inc(once("mem_stat")[0], 1)
            run(from_h("cross", 0, 1))
            pe.wait_ge(*once("mem_std"))
            pe.wait_ge(*norm_event("n4", "std", 1))

            def from_mem(h, j):
                return product("cross", h, j, lambda k: MEMC[0][:, k, :], lambda k: MEMC[1][:, k, :], n=MEM)

            for j in range(4):
                run(from_mem(0, 2 + j))

            def cross(h, steps):
                for j in (4, 5):
                    s, c = units.use("cross", h, j)
                    pe.wait_ge(S_[f"taken{s}"], c)
                pe.wait_ge(S_["x_out_lo"], 2 * h + 1)
                pe.wait_ge(S_["x_out_lo"], 2 * h + 2)
                for mb in range(2):
                    for c in range(2):
                        last = nc.tensor.transpose(OUTB[:, (2 * mb + c) * P:(2 * mb + c + 1) * P],
                                                   XV[:, c, mb * P:(mb + 1) * P], ident[:])
                last.then_inc(S_["x_vt"], 1)
                pe.wait_ge(S_["x_q_hi"], 2 * h + 2)
                pe.wait_ge(S_["x_q_lo"], 2 * h + 2)
                pe.wait_ge(S_["x_k_hi"], h + 1)
                pe.wait_ge(S_["x_k_lo"], h + 1)
                for i in range(NB):
                    if i < 2:
                        pe.wait_ge(S_["x_pt_lo"], 2 * h + 1 + i)
                    else:
                        pe.wait_ge(S_["x_exp"], 4 * h + i - 1)
                    bank = WORK[i % 2][:, 0:MEM]
                    for c in range(2):
                        for q, k in ((0, 0), (0, 1), (1, 0)):
                            last = mm(bank, XQC[q][:, c, i * P:(i + 1) * P], XKC[k][:, c, :],
                                      start=(c == q == k == 0), stop=(c == q == 1))
                    last.then_inc(S_["x_score"], 1)
                    run(steps, 16)
                pe.wait_ge(S_["x_probs"], 4 * h + 4)
                for mb in range(2):
                    for i in range(NB):
                        last = nc.tensor.transpose(WORK[mb][:, i * P:(i + 1) * P], XPR[:, i, mb * P:(mb + 1) * P],
                                                   ident[:])
                    last.then_inc(S_["x_pt"], 1)
                    run(steps, 16)
                pe.wait_ge(S_["x_v_hi"], h + 1)
                pe.wait_ge(S_["x_v_lo"], h + 1)
                for mb in range(2):
                    pe.wait_ge(S_["x_pt_hi"], 2 * h + mb + 1)
                    pe.wait_ge(S_["x_pt_lo"], 2 * h + mb + 3)
                    for c, bank in enumerate((OUTB, STAT)):
                        for v, p in ((0, 0), (0, 1), (1, 0)):
                            last = mm(bank[:], XVC[v][:, mb, c * P:(c + 1) * P], XTC[p][:, mb, :],
                                      start=(mb == v == p == 0), stop=(mb == v == 1), skip_group_check=True)
                last.then_inc(S_["x_pv"], 1)
                run(steps)

            with pe.Fori(0, 3) as h:
                cross(h, chain(*[from_h("cross", h + 1, j) for j in range(2)],
                               *[from_mem(h + 1, 2 + j) for j in range(4)]))
            cross(3, chain())
            for e in range(DC):
                run(from_pair("xout", e // 4, e % 4, XO, cut_pair("x_out_hi", "x_out_lo", 2) if e == 0 else None))

            def ffn_group(name, g, first=False):
                wide = len(units.slots[name]) // 2 - 4
                for j in range(2 * wide):
                    run(from_h(name, g, j, cut_of("n5") if first and j == 0 else None))
                    if first and j == 0:
                        norm_stat("n5", "n4")
                base = 16 if name == "ffn_tail" else 8 * g
                for j in range(DC):
                    run(from_pair(name, g, 2 * wide + j, FF, cut_pair("ff_hi", "ff_lo", base) if j == 0 else None))
                    if name == "ffn_tail" and j:
                        back(j - 1)
                if name == "ffn_tail":
                    back(DC - 1)

            def back(e):
                if e >= 2:
                    pe.wait_ge(S_["y_taken"], e - 1)
                pe.wait_ge(S_["y_gained"], e + 1)
                for t in range(NB):
                    last = nc.tensor.transpose(WORK[e % 2][:, t * P:(t + 1) * P], YG[:, e % 2, t * P:(t + 1) * P],
                                               ident[:])
                last.then_inc(S_["y_t"], 1)

            ffn_group("ffn", 0, True)
            ffn_group("ffn", 1)
            ffn_group("ffn_tail", 0)

            pe.wait_ge(*norm_event("n6", "acc", DC + 1))
            for t in range(NB):
                last = mm(STAT[:, t:t + 1], ACC1[:, t * P:(t + 1) * P], ones[:, 0:1], start=True, stop=True)
            last.then_inc(norm_event("n6", "stat", 0)[0], 1)

        @block.scalar
        def _(act):
            A = nc.scalar.activation
            own = Chain(act, S_["act_own"])

            def norm_chunk(tag, e, parity):
                x_e = X[:, bass.ds(e, 1), :]
                A(HH[:, bass.ds(e, 1), :], x_e, ACT.Copy, scale=par(GAIN[tag], e)).then_inc(norm_event(tag, "hh", 0)[0], 1)
                act.wait_ge(*norm_event(tag, "acc", e + 1))
                A(SQS[tag][:, parity:parity + 1, :], x_e, ACT.Square).then_inc(norm_event(tag, "sq", 0)[0], 1)

            def norm_root(tag):
                act.wait_ge(*norm_event(tag, "stat", 1))
                A(STD[tag][:], STAT[:], ACT.Sqrt, bias=EPSC[:], scale=1.0 / D).then_inc(norm_event(tag, "std", 0)[0], 1)

            def rsqrt_stat(tag, n, scale, dst):
                act.wait_ge(S_[tag + "_stat"], n + 1)
                own.link(A(dst, STAT[:], ACT.Ln, bias=EPSC[:], scale=scale))
                A(dst, dst, ACT.Exp, scale=-0.5).then_inc(S_[tag + "_stat_read"], 1)

            def probs_hi(tag, M, kind, h, n):
                wide = len(kind.queries(kind.jobs[n][1])) * P
                act.wait_ge(S_[tag + "_pt"], h * len(kind.jobs) + n + 1)
                A(M["TH"][:, n % 2, 0:wide], WORK[n % 2][:, 0:wide], ACT.Copy).then_inc(S_[tag + "_pt_hi"], 1)

            def exps(tag, M, kind, h, v_hi, after=None):
                for t in range(8):
                    part, i = t % 2, t // 2
                    wide = (i + 1 - kind.first(i)) * P
                    act.wait_ge(S_[tag + "_row_max"], h * 8 + t + 1)
                    A(M["PR"][:, part, kind.offset(i):kind.offset(i) + wide], WORK[t % 2][:, 0:wide], ACT.Exp,
                      bias=NMAX[:, t:t + 1], accum_out=SUM[:, t:t + 1]).then_inc(S_[tag + "_exp"], 1)
                    if t == 0:
                        act.wait_ge(S_[tag + "_vt"], h + 1)
                        v_hi()
                    if after:
                        after(t)

            for e in range(DC + 2):
                if e < DC:
                    act.wait_ge(S_["xt_done"], e + 1)
                    A(X[:, e, :], WORK[e % 2][:], ACT.Copy).then_inc(S_["n1_x"], 1)
                if e == 2:
                    act.wait_ge(*once("gain_taken"))
                if e >= 2:
                    act.wait_ge(S_["n1_x"], e - 1)
                    norm_chunk("n1", e - 2, e % 2)
            norm_root("n1")
            act.preload_act_table_set("natural_log_exp_and_others")
            act.wait_ge(*once("lam_dots"))
            A(LAMS[:, 2:4], LAMS[:, 0:2], ACT.Exp).then_inc(once("lam_exp")[0], 1)
            act.wait_ge(*once("decay_abs"))
            A(LOGT[:, 1, :], LOGT[:, 0, :], ACT.Exp, scale=-1.0).then_inc(once("decay_exp")[0], 1)

            def load_bias1(h):
                act.wait_ge(S_["tiles_stored"], 64)
                for t, tile in ((tiles1[0], BIASH), (tiles1[1], BIASL)):
                    act.dma_start(tile[:].bitcast(F32), t[bass.ds(h, 1), :, :].rearrange("o p t -> (o p) t")
                                  ).then_inc(S_["bias_landed"], 16)


            def square1(h, side):
                s, c = units.use("qkv", h, side)
                act.wait_ge(S_[f"taken{s}"], c)
                A(M1["SQ"][:, side, :], M1["QN"][:, side, :], ACT.Square).then_inc(S_["a_qk_sq"], 1)

            def qk_hi1(h, side):
                act.wait_ge(S_["a_qk_norm"], 2 * h + 1 + side)
                A(M1["QH"][:, side, :], M1["QN"][:, side, :], ACT.Copy).then_inc(S_["a_qk_hi"], 1)

            square1(0, 0)
            square1(0, 1)
            rsqrt_stat("a", 0, 1.0 / 64, M1["RQ"][:, 0, :])
            rsqrt_stat("a", 1, 1.0 / 64, M1["RQ"][:, 1, :])
            qk_hi1(0, 0)
            qk_hi1(0, 1)

            def head1(h, last):
                def v_hi():
                    A(M1["VH"][:, 0], OUTB[:].rearrange("p (j e) -> p j e", j=NB), ACT.Copy
                      ).then_inc(S_["a_v_hi"], 1)

                exps("a", M1, KIND1, h, v_hi, None if last else lambda t: square1(h + 1, 0) if t == 5 else None)
                if not last:
                    load_bias1(h + 1)
                    square1(h + 1, 1)
                for n in range(4):
                    probs_hi("a", M1, KIND1, h, n)
                    if n == 1 and not last:
                        rsqrt_stat("a", 3 * h + 2, 1.0 / 64, M1["RQ"][:, 0, :])
                        rsqrt_stat("a", 3 * h + 3, 1.0 / 64, M1["RQ"][:, 1, :])
                    if n >= 2 and not last:
                        qk_hi1(h + 1, n - 2)
                act.wait_ge(S_["a_out_taken"], h + 2)
                A(M1["SQ"][:, 2, :], M1["OR"][:], ACT.Square).then_inc(S_["a_o_sq"], 1)
                rsqrt_stat("a", 3 * h + (2 if last else 4), 1.0 / P, M1["RQ"][:, 2, :])
                act.wait_ge(S_["a_o_norm"], h + 1)
                A(AO[0][:, bass.ds(h, 1), :], M1["OR"][:].unsqueeze(1), ACT.Copy).then_inc(S_["a_o_hi"], 1)

            with act.Fori(0, HEADS - 1) as h:
                own.enter(h, 3)
                head1(h, False)
                own.leave(HEADS - 1)
            head1(HEADS - 1, True)

            def conv_hi(n):
                act.wait_ge(S_["xc_raw"], n + 1)
                A(XCH[:], XC[:], ACT.Copy).then_inc(S_["xc_hi"], 1)

            def rnn(n, last):
                s, c = units.use("rnn_last", 0, 0) if last else units.use("rnn", n, 0)
                act.wait_ge(S_[f"taken{s}"], c)
                A(G2[:], GT[:], ACT.Square).then_inc(S_["g2"], 1)
                s, c = units.use("rnn_last", 0, 1) if last else units.use("rnn", n, 2)
                act.wait_ge(S_[f"product{s}"], c)
                A(RT[:], psum[s][:], ACT.Tanh, bias=small[:, bass.ds(HBA + n, 1)], scale=0.5
                  ).then_inc(S_["gate_tanh"], 1)
                A(IT[:], WORK[0][:], ACT.Tanh, bias=small[:, bass.ds(HBX + n, 1)], scale=0.5
                  ).then_inc(S_["gate_tanh"], 1)
                act.wait_ge(S_["gelu_arg"], n + 1)
                A(G2[:], G2[:], ACT.Tanh, scale=math.sqrt(2 / math.pi)).then_inc(S_["gelu_tanh"], 1)
                act.wait_ge(S_["gate_tanh"], 2 * n + 2)
                own.mark(A(TT[:], RT[:], ACT.Tanh, bias=small[:, bass.ds(HZC + n, 1)],
                           scale=small[:, bass.ds(HZC + n, 1)]))
                A(AT[:], RT[:], ACT.Exp, bias=small[:, bass.ds(NZC + n, 1)], scale=small[:, bass.ds(NZC + n, 1)]
                  ).then_inc(S_["decay"], 1)
                act.preload_act_table(ACT.Sqrt)
                if not last:
                    conv_hi(n + 1)
                own.wait()
                A(MT[:], TT[:], ACT.Sqrt).then_inc(S_["root"], 1)
                if not last:
                    act.preload_act_table(ACT.Tanh)
                act.wait_ge(S_["ro_raw"], n + 1)
                A(RO[0][:, bass.ds(n, 1), :], HS[:].unsqueeze(1), ACT.Copy).then_inc(S_["ro_hi"], 1)

            conv_hi(0)
            with act.Fori(0, DC - 1) as n:
                own.enter(n, 1)
                rnn(n, False)
                own.leave(DC - 1)
            rnn(DC - 1, True)

            act.preload_act_table(ACT.Sigmoid)
            with act.Fori(0, DC) as e:
                for j in range(2):
                    s, c = units.use("merge1", e, 1 + j)
                    act.wait_ge(S_[f"taken{s}"], c)
                    A(SG[:, j, :], GA[:, j, :], ACT.Sigmoid).then_inc(S_["sg"], 1)
            for e in range(DC):
                act.wait_ge(S_["mg"], DC)
                A(AO[0][:, e, :], MG[:, e, :], ACT.Copy).then_inc(S_["mg_hi"], 1)
            act.preload_act_table(ACT.Sqrt)
            act.wait_ge(*norm_event("n2", "acc", 1))
            for i in range(2):
                for j in range(4):
                    s, c = units.use("out1", i, j)
                    act.wait_ge(S_[f"taken{s}"], c)
                    norm_chunk("n2", 4 * i + j, j % 2)
            norm_root("n2")

            def squares(g, first):
                for j in range(8):
                    s, c = units.use("mlp", g, j)
                    act.wait_ge(S_[f"taken{s}"], c)
                    if not first or j >= 2:
                        act.wait_ge(S_["u_lo"], 8 * g + j - 1)
                    A(SU[:, j % 2, :], TU[:, j % 2, :], ACT.Square).then_inc(S_["u_sq"], 1)
                    act.wait_ge(S_["u_sq"], 8 * g + j + 1)
                    A(UH[:, j, :], SU[:, j % 2, :], ACT.Copy).then_inc(S_["u_hi"], 1)

            squares(0, True)
            with act.Fori(1, 3) as g:
                squares(g, False)
            squares(3, False)

            def norm_chunks(tag, name, it, first, after=None):
                for e in range(DC):
                    wide = len(units.slots[name])
                    s, c = units.use(name, it + (first + e) // wide, (first + e) % wide)
                    act.wait_ge(S_[f"taken{s}"], c)
                    norm_chunk(tag, e, e % 2)
                    if after:
                        after(e)

            norm_chunks("n3", "mlp", 3, 8)
            norm_root("n3")

            act.preload_act_table_set("natural_log_exp_and_others")
            act.wait_ge(*once("forget_abs"))
            A(FE[:], FA[:], ACT.Exp, scale=-1.0).then_inc(once("forget_exp")[0], 1)
            act.wait_ge(*once("forget_one_plus"))
            A(FLN[:], FU[:], ACT.Ln).then_inc(once("forget_ln")[0], 1)
            act.wait_ge(*once("forget_cum"))
            A(FCH[:], FT[:], ACT.Copy).then_inc(once("forget_cum_hi")[0], 1)

            def qk_hi2(tag, name, h, j, side, n):
                s, c = units.use(name, h, j)
                act.wait_ge(S_[f"taken{s}"], c)
                A(M2["QH"][:, side, :], M2["QN"][:, side, :], ACT.Copy).then_inc(S_[tag + "_qk_hi"], 1)

            def v_hi2(tag):
                for part in range(2):
                    cols = slice(64 * part, 64 * part + 64)
                    A(M2["VH"][:, part, :, cols], OUTB[:].rearrange("p (j e) -> p j e", j=NB)[:, :, cols], ACT.Copy
                      ).then_inc(S_[tag + "_v_hi"], 1)

            def out_hi2(tag, Y, h, first=0):
                act.wait_ge(S_[tag + "_pv"], first + h + 1)
                A(Y[0][:, bass.ds(h, 1), :], OUTB[:].unsqueeze(1), ACT.Copy).then_inc(S_[tag + "_o_hi"], 1)

            act.wait_ge(*once("values_cleared"))
            for side in range(2):
                qk_hi2("f", "fox", 0, side, side, side)

            def fox(h, last):
                exps("f", M2, KIND_FOX, h, lambda: v_hi2("f"))
                for n in range(8):
                    probs_hi("f", M2, KIND_FOX, h, n)
                    if n in (1, 3):
                        qk_hi2("f", *(("swa_first", 0) if last else ("fox", h + 1)), n // 2, n // 2, 0)
                out_hi2("f", YF, h)

            with act.Fori(0, 3) as h:
                fox(h, False)
            fox(3, True)

            def load_bias2(h):
                act.wait_ge(S_["tiles_stored"], 96)
                for k in range(2):
                    for part in range(2):
                        act.dma_start(BIAS2[k][:, part, :].bitcast(F32),
                                      tiles2[k][bass.ds(h + 4 * part, 1), :, :].rearrange("o p t -> (o p) t")
                                      ).then_inc(S_["bias2_landed"], 16)

            load_bias2(0)
            act.wait_ge(S_["f_vt"], 5)
            v_hi2("f")

            def swa(h, last):
                for t in range(8):
                    part, i = t % 2, t // 2
                    wide = (i + 1 - KIND_SWA.first(i)) * P
                    act.wait_ge(S_["f_row_max"], 8 * h + t + 33)
                    A(M2["PR"][:, part, KIND_SWA.offset(i):KIND_SWA.offset(i) + wide], WORK[t % 2][:, 0:wide], ACT.Exp,
                      bias=NMAX[:, t:t + 1], accum_out=SUM[:, t:t + 1]).then_inc(S_["f_exp"], 1)
                    A(SEXP[:, t:t + 1], small[:, bass.ds(SINK + 4 * part + h, 1)], ACT.Exp, bias=NMAX[:, t:t + 1]
                      ).then_inc(S_["s_sink"], 1)
                if not last:
                    load_bias2(h + 1)
                for n in range(8):
                    probs_hi("f", M2, KIND_SWA, h + 4, n)
                    if n == 1 and not last:
                        qk_hi2("f", "swa", h, 0, 0, 0)
                act.wait_ge(S_["yc_raw"], h + 1)
                A(YC[0][:, bass.ds(h, 1), :], CV.unsqueeze(1), ACT.Copy).then_inc(S_["yc_hi"], 1)
                out_hi2("f", YS, h, 4)

            with act.Fori(0, 3) as h:
                swa(h, False)
            swa(3, True)

            act.preload_act_table(ACT.Sigmoid)
            with act.Fori(0, DC) as e:
                for j in range(3):
                    s, c = units.use("merge2", e, 1 + j)
                    act.wait_ge(S_[f"taken{s}"], c)
                    A(SG2[:, j, :], GA2[:, j, :], ACT.Sigmoid).then_inc(S_["sg2"], 1)
                act.wait_ge(S_["mgc_raw"], e + 1)
                A(MGC[0][:, bass.ds(e, 1), :], MX[:, 0:1, :], ACT.Copy).then_inc(S_["mgc_hi"], 1)

            act.preload_act_table(ACT.Sqrt)
            def mem_chunks(e):
                for m in mem_after(e):
                    act.wait_ge(S_["mem_t"], m + 1)
                    A(MEMC[0][:, m, :], WORK[m % 2][:, 0:MEM], ACT.Copy, scale=par("mem_norm_g_2", m)
                      ).then_inc(S_["mem_hi"], 1)
                    act.wait_ge(S_["mem_acc"], m + 1)
                    A(SQM[:, m % 2, :], WORK[m % 2][:, 0:MEM], ACT.Square).then_inc(S_["mem_sq"], 1)

            norm_chunks("n4", "out2", 0, 0, mem_chunks)
            norm_root("n4")
            act.wait_ge(*once("mem_stat"))
            A(STDM[:], OUTB[:, 0:MEM], ACT.Sqrt, bias=EPSC[:], scale=1.0 / D).then_inc(once("mem_std")[0], 1)
            act.preload_act_table(ACT.Exp)

            def cross_cut(h):
                for j in range(2):
                    s, c = units.use("cross", h, j)
                    act.wait_ge(S_[f"taken{s}"], c)
                    A(XQC[0][:, j, :], XQ[:, j, :], ACT.Copy).then_inc(S_["x_q_hi"], 1)
                for j in (2, 3):
                    s, c = units.use("cross", h, j)
                    act.wait_ge(S_[f"taken{s}"], c)
                A(XKC[0][:], XK[:], ACT.Copy).then_inc(S_["x_k_hi"], 1)

            cross_cut(0)

            def cross(h, last):
                act.wait_ge(S_["x_vt"], h + 1)
                A(XVC[0][:], OUTB[:].rearrange("p (m e) -> p m e", m=2), ACT.Copy).then_inc(S_["x_v_hi"], 1)
                for i in range(NB):
                    act.wait_ge(S_["x_row_max"], 4 * h + i + 1)
                    A(XPR[:, i, :], WORK[i % 2][:, 0:MEM], ACT.Exp, bias=NMAX[:, i:i + 1], accum_out=SUM[:, i:i + 1]
                      ).then_inc(S_["x_exp"], 1)
                for mb in range(2):
                    act.wait_ge(S_["x_pt"], 2 * h + mb + 1)
                    A(XTC[0][:, mb, :], WORK[mb][:], ACT.Copy).then_inc(S_["x_pt_hi"], 1)
                if not last:
                    cross_cut(h + 1)
                act.wait_ge(S_["x_pv"], h + 1)
                for c, bank in enumerate((OUTB, STAT)):
                    A(XO[0][:, bass.ds(2 * h + c, 1), :], bank[:].unsqueeze(1), ACT.Copy
                      ).then_inc(S_["x_out_hi"], 1)

            act.sem_inc(S_["x_out_hi"], 2)
            with act.Fori(0, 3) as h:
                cross(h, False)
            cross(3, True)
            act.preload_act_table(ACT.Sqrt)
            norm_chunks("n5", "xout", 0, 0)
            norm_root("n5")

            act.preload_act_table(ACT.Silu)

            def ffn_group(name, g):
                wide = len(units.slots[name]) // 2 - 4
                base = 16 if name == "ffn_tail" else 8 * g
                for j in range(wide):
                    s, c = units.use(name, g, 2 * j)
                    act.wait_ge(S_[f"taken{s}"], c)
                    A(FGA[:, j % 2, :], FGA[:, j % 2, :], ACT.Silu).then_inc(S_["ff_silu"], 1)
                    act.wait_ge(S_["ff_raw"], base + j + 1)
                    A(FF[0][:, j, :], FUP[:, j % 2, :], ACT.Copy).then_inc(S_["ff_hi"], 1)

            ffn_group("ffn", 0)
            ffn_group("ffn", 1)
            ffn_group("ffn_tail", 0)
            act.preload_act_table(ACT.Sqrt)
            for e in range(DC):
                s, c = units.use("ffn_tail", 0, 12 + e)
                act.wait_ge(S_[f"taken{s}"], c)
                if e >= 2:
                    act.wait_ge(S_["y_t"], e - 1)
                A(YG[:, e % 2, :], X[:, e, :], ACT.Copy, scale=par("final_norm_g_2", e)).then_inc(S_["y_gained"], 1)
                act.wait_ge(*norm_event("n6", "acc", e + 1))
                A(SQ1[:, e % 2, :], X[:, e, :], ACT.Square).then_inc(norm_event("n6", "sq", 0)[0], 1)
            act.wait_ge(*norm_event("n6", "stat", 1))
            A(RS[:, 0:NB], STAT[:, 0:NB], ACT.Sqrt, bias=EPSC[:], scale=1.0 / D).then_inc(norm_event("n6", "std", 0)[0], 1)
            act.wait_ge(S_["y_rstd"], 1)
            act.wait_ge(S_["y_taken"], DC)
            for t in range(1, NB, 2):
                A(YTOK[:, t, :], YTOK[:, t, :], ACT.Copy, scale=NMAX[:, t:t + 1]).then_inc(S_["y_scaled_a"], 1)

        @block.vector
        def _(dve):
            V = nc.vector
            own = Chain(dve, S_["dve_own"])
            for s in range(SLOTS):
                dve.sem_inc(S_[f"taken{s}"], 1)
            for name in ("a_pt_lo", "a_out_taken", "f_pt_lo", "f_out_taken",
                         "m2_fox_taken", "x_pt_lo", "x_pt_lo", "x_out_lo", "x_out_lo"):
                dve.sem_inc(S_[name], 1)

            def take(name, it, j, op):
                s, c = units.use(name, it, j)
                dve.wait_ge(S_[f"product{s}"], c)
                ins = op(psum[s])
                ins.then_inc(S_[f"taken{s}"], 1)
                return ins

            def norm_chunk(tag, e, parity):
                dve.wait_ge(*norm_event(tag, "hh", e + 1))
                V.scalar_tensor_tensor(HL[:, bass.ds(e, 1), :], X[:, bass.ds(e, 1), :], par(GAIN[tag], e),
                                       HH[:, bass.ds(e, 1), :].bitcast(F32), ALU.mult, ALU.subtract
                                       ).then_inc(norm_event(tag, "hl", 0)[0], 1)
                dve.wait_ge(*norm_event(tag, "sq", e + 1))
                dve.wait_ge(*norm_event(tag, "acc", e + 1))
                V.tensor_tensor(ACC[tag][:], ACC[tag][:], SQS[tag][:, parity, :], ALU.add
                                ).then_inc(norm_event(tag, "acc", 0)[0], 1)

            def norm_rstd(tag):
                dve.wait_ge(*norm_event(tag, "std", 1))
                own.link(V.reciprocal(RSTD[:], STD[tag][:]))

            def probs_lo(tag, M, kind, h, n):
                wide = len(kind.queries(kind.jobs[n][1])) * P
                dve.wait_ge(S_[tag + "_pt_hi"], h * len(kind.jobs) + n + 1)
                V.tensor_tensor(M["TL"][:, n % 2, 0:wide], WORK[n % 2][:, 0:wide],
                                M["TH"][:, n % 2, 0:wide].bitcast(F32), ALU.subtract).then_inc(S_[tag + "_pt_lo"], 1)

            def softmax(tag, M, kind, h, row_max, v_lo, combine, between=None):
                for i in range(NB):
                    for part in range(2):
                        t = 2 * i + part
                        wide = (i + 1 - kind.first(i)) * P
                        dve.wait_ge(S_[tag + "_score"], h * 8 + t + 1)
                        row_max(t, part, WORK[t % 2][:, 0:wide]).then_inc(S_[tag + "_row_max"], 1)
                        if t == 0 and kind is not KIND_SWA:
                            dve.wait_ge(S_[tag + "_v_hi"], h + 1 if tag == "a" else 2 * h + 2)
                            v_lo()
                    if i:
                        dve.wait_ge(S_[tag + "_exp"], h * 8 + 2 * i)
                        combine(i - 1).then_inc(S_[tag + "_probs"], 1)
                    if between:
                        between(i)
                dve.wait_ge(S_[tag + "_exp"], h * 8 + 8)
                combine(NB - 1).then_inc(S_[tag + "_probs"], 1)

            V.memset(TAB[BUCKETS:BUCKETS + 1, :, :], MASKED).then_inc(once("tab_masked")[0], 1)
            own.mark(V.memset(halves[:], 0.0))
            own.mark(V.memset(SROW[:, 8:16], 0.0))
            own.mark(V.memset(EPSC[:], EPS))
            own.mark(V.memset(IND[:], 0.0))
            own.mark(V.memset(SIDE[:], 0.0))
            V.memset(ACC0[:], 0.0).then_inc(norm_event("n1", "acc", 0)[0], 1)
            own.wait()
            own.mark(V.memset(halves[0:64, 0:64], 1.0))
            own.mark(V.memset(halves[64:128, 64:128], 1.0))
            own.mark(V.memset(SIDE[0:64, 0:1], 1.0))
            own.mark(V.memset(SIDE[64:128, 1:2], -1.0))
            dve.wait_ge(*once("ident_made"))
            for q in range(4):
                own.mark(V.tensor_copy(IND[32 * q:32 * q + 8, :], ident[32 * q:32 * q + 8, 32 * q:32 * q + 8]))
            own.link(V.tensor_copy(identr[:], ident[:]))
            dve.wait_ge(*once("gain_done"))
            V.tensor_copy(PARAM[:, 0:8], OUTB[:, 0:8]).then_inc(once("gain_taken")[0], 1)
            dve.wait_ge(*once("gain_taken"))
            for e in range(DC):
                norm_chunk("n1", e, e % 2)
                if e == 2:
                    dve.wait_ge(*once("par_done"))
                    own.mark(V.tensor_copy(PARAM[:, 8:80], OUTB[:, 8:80]))
                    own.link(V.tensor_copy(PARAM[:, 96:151], OUTB[:, 96:151]))
                    V.tensor_scalar(LOGT[:, 2, :], PARAM[:, column["lru_lambda"]:column["lru_lambda"] + 8],
                                    -1.0, None, ALU.mult).then_inc(once("par_taken")[0], 1)
                    own.mark(V.tensor_scalar(small[:, HBA:HBA + 16], PARAM[:, column["b_rg_a"]:column["b_rg_a"] + 16],
                                             0.5, None, ALU.mult))
                    own.mark(V.tensor_scalar(small[:, QG8:QG8 + 1], PARAM[:, QG:QG + 1], 64 ** -0.5, None, ALU.mult))
                    own.mark(V.tensor_scalar(small[:, SUBL:SUBL + 1], PARAM[:, SUBG:SUBG + 1], 1 - LAMBDA_INIT, None,
                                             ALU.mult))
                if e == 4:
                    dve.wait_ge(*once("brow_done"))
                    parts = ((0, 512, psum[3][0:8, :]), (512, 512, psum[2][0:8, :]))
                    for at, wd, bank in parts:
                        own.mark(V.tensor_copy(BROWH[:, at:at + wd], bank))
                    own.wait()
                    for at, wd, bank in parts:
                        ins = V.tensor_tensor(BROWL[:, at:at + wd], bank, BROWH[:, at:at + wd].bitcast(F32),
                                              ALU.subtract)
                        if at == 0:
                            own.link(ins)
                    ins.then_inc(once("brow_rows")[0], 1)
            dve.wait_ge(*once("par_taken"))
            V.tensor_tensor(LOGT[:, 0, :], LOGT[:, 2, :], PARAM[:, column["lru_lambda"]:column["lru_lambda"] + 8],
                            ALU.max).then_inc(once("decay_abs")[0], 1)
            dve.wait_ge(S_["lam_landed"], 96)
            own.mark(V.tensor_tensor(LAM[:, 0, :], LAM[:, 0, :], LAM[:, 1, :], ALU.mult))
            own.link(V.tensor_tensor(LAM[:, 2, :], LAM[:, 2, :], LAM[:, 3, :], ALU.mult))
            own.mark(V.tensor_reduce(LAMS[:, 0:1], LAM[:, 0, :], AX.X, ALU.add))
            V.tensor_reduce(LAMS[:, 1:2], LAM[:, 2, :], AX.X, ALU.add).then_inc(once("lam_dots")[0], 1)
            own.wait()
            norm_rstd("n1")

            def scaled(dst):
                return lambda bank: V.tensor_tensor(dst, bank[:], RSTD[:], ALU.mult)

            def take_qk1(h, side):
                take("qkv", h, side, scaled(M1["QN"][:, side, :]))

            def norm_qk1(h, n, side):
                dve.wait_ge(S_["a_stat_read"], n + 1)
                gain = small[:, QG8:QG8 + 1] if side == 0 else PARAM[:, KG:KG + 1]
                V.scalar_tensor_tensor(M1["QN"][:, side, :], M1["QN"][:, side, :], gain, M1["RQ"][:, side, :],
                                       ALU.mult, ALU.mult).then_inc(S_["a_qk_norm"], 1)

            def qk_lo(tag, M, h, side):
                dve.wait_ge(S_[tag + "_qk_hi"], 2 * h + 1 + side)
                V.tensor_tensor(M["QL"][:, side, :], M["QN"][:, side, :], M["QH"][:, side, :].bitcast(F32),
                                ALU.subtract).then_inc(S_[tag + "_qk_lo"], 1)

            def v_lo1():
                V.tensor_tensor(M1["VL"][:, 0], OUTB[:].rearrange("p (j e) -> p j e", j=NB),
                                M1["VH"][:, 0].bitcast(F32), ALU.subtract).then_inc(S_["a_v_lo"], 1)

            def row_max1(t, part, bank):
                return V.tensor_reduce(NMAX[:, t:t + 1], bank, AX.X, ALU.max, negate=True)

            def combine1(i):
                at, wide = KIND1.offset(i), (i + 1) * P
                p0, p1 = M1["PR"][:, 0, at:at + wide], M1["PR"][:, 1, at:at + wide]
                own.link(V.reciprocal(RS[:, 2 * i:2 * i + 2], SUM[:, 2 * i:2 * i + 2]))
                own.link(V.tensor_scalar(p1, p1, RS[:, 2 * i + 1:2 * i + 2], small[:, LAMC:LAMC + 1],
                                         ALU.mult, ALU.mult))
                return V.scalar_tensor_tensor(p0, p0, RS[:, 2 * i:2 * i + 1], p1, ALU.mult, ALU.add)

            take_qk1(0, 0)
            dve.wait_ge(*once("lam_exp"))
            own.link(V.tensor_tensor(LAMS[:, 4:5], LAMS[:, 3:4], LAMS[:, 2:3], ALU.subtract))
            V.tensor_scalar(SROW[:, 8:9], LAMS[:, 4:5], -LAMBDA_INIT, None, ALU.add).then_inc(once("lam_row")[0], 1)
            take_qk1(0, 1)
            dve.wait_ge(*once("decay_exp"))
            own.link(V.tensor_scalar(LOGT[:, 3, :], LOGT[:, 1, :], 2.0, None, ALU.add))
            own.link(V.reciprocal(LOGT[:, 3, :], LOGT[:, 3, :]))
            own.link(V.tensor_tensor(LOGT[:, 3, :], LOGT[:, 3, :], LOGT[:, 1, :], ALU.mult))
            own.link(V.tensor_tensor(LOGT[:, 4, :], LOGT[:, 3, :], LOGT[:, 3, :], ALU.mult))
            own.link(V.tensor_scalar(LOGT[:, 5, :], LOGT[:, 4, :], 1 / 17, 1 / 15, ALU.mult, ALU.add))
            for k in (13, 11, 9, 7, 5, 3, 1):
                own.link(V.tensor_tensor(LOGT[:, 5, :], LOGT[:, 5, :], LOGT[:, 4, :], ALU.mult))
                own.link(V.tensor_scalar(LOGT[:, 5, :], LOGT[:, 5, :], 1 / k, None, ALU.add))
            own.link(V.tensor_tensor(LOGT[:, 5, :], LOGT[:, 5, :], LOGT[:, 3, :], ALU.mult))
            own.link(V.tensor_scalar(LOGT[:, 2, :], LOGT[:, 2, :], 0.0, None, ALU.max))
            own.link(V.scalar_tensor_tensor(LOGT[:, 2, :], LOGT[:, 5, :], 2.0, LOGT[:, 2, :], ALU.mult, ALU.add))
            own.mark(V.tensor_scalar(small[:, HZC:HZC + 8], LOGT[:, 2, :], 2.0, None, ALU.mult))
            own.link(V.tensor_scalar(small[:, NZC:NZC + 8], LOGT[:, 2, :], -4.0, None, ALU.mult))
            for side in range(2):
                norm_qk1(0, side, side)
            for side in range(2):
                qk_lo("a", M1, 0, side)
            take("qkv", 0, 2, scaled(M1["VR"][:]))
            dve.wait_ge(*once("lam_done"))
            own.mark(V.tensor_copy(small[:, SINK:SINK + 8], psum[3][:, 0:8]))
            own.mark(V.tensor_scalar(small[:, NSINK:NSINK + 8], psum[3][:, 0:8], -1.0, None, ALU.mult))
            V.tensor_copy(small[:, LAMC:LAMC + 1], psum[3][:, 8:9]).then_inc(once("lam_taken")[0], 1)
            own.wait()
            dve.wait_ge(*once("lam_taken"))

            def head1(h, last):
                def between(i):
                    if i == 1 and not last:
                        take_qk1(h + 1, 0)

                softmax("a", M1, KIND1, h, row_max1, v_lo1, combine1, between)
                if not last:
                    take_qk1(h + 1, 1)
                for n in range(4):
                    probs_lo("a", M1, KIND1, h, n)
                    if n == 1 and not last:
                        for side in range(2):
                            norm_qk1(h + 1, 3 * h + 2 + side, side)
                    if n >= 2 and not last:
                        qk_lo("a", M1, h + 1, n - 2)
                dve.wait_ge(S_["a_pv"], h + 1)
                V.tensor_copy(M1["OR"][:], OUTB[:]).then_inc(S_["a_out_taken"], 1)
                if not last:
                    take("qkv", h + 1, 2, scaled(M1["VR"][:]))
                dve.wait_ge(S_["a_stat_read"], 3 * h + (3 if last else 5))
                dve.wait_ge(S_["a_o_sq"], h + 1)
                V.scalar_tensor_tensor(M1["OR"][:], M1["OR"][:], small[:, SUBL:SUBL + 1], M1["RQ"][:, 2, :],
                                       ALU.mult, ALU.mult).then_inc(S_["a_o_norm"], 1)
                dve.wait_ge(S_["a_o_norm"], h + 1)
                dve.wait_ge(S_["a_o_hi"], h + 1)
                V.tensor_tensor(AO[1][:, bass.ds(h, 1), :], M1["OR"][:].unsqueeze(1),
                                AO[0][:, bass.ds(h, 1), :].bitcast(F32), ALU.subtract).then_inc(S_["a_o_lo"], 1)

            with dve.Fori(0, HEADS - 1) as h:
                own.enter(h, 8)
                head1(h, False)
                own.leave(HEADS - 1)
            head1(HEADS - 1, True)


            def conv1(n, unit):
                take(*unit, lambda bank: V.tensor_tensor(XR[:, 3:S + 3], bank[:], RSTD[:], ALU.mult))
                s, c = units.use(*unit)
                dve.wait_ge(S_[f"taken{s}"], c)
                own.link(V.tensor_scalar(XC[:], XR[:, 0:S], par("conv_w", n), par("conv_b", n), ALU.mult, ALU.add))
                for tap in (1, 2, 3):
                    ins = V.scalar_tensor_tensor(XC[:], XR[:, tap:tap + S], par("conv_w", n + DC * tap), XC[:],
                                                 ALU.mult, ALU.add)
                    if tap < 3:
                        own.link(ins)
                ins.then_inc(S_["xc_raw"], 1)
                dve.wait_ge(S_["xc_hi"], n + 1)
                V.tensor_tensor(XCL[:], XC[:], XCH[:].bitcast(F32), ALU.subtract).then_inc(S_["xc_lo"], 1)

            def rnn(n, last):
                gates = ("rnn_last", 0, 1) if last else ("rnn", n, 2)
                take(*(("rnn_last", 0, 0) if last else ("rnn", n, 0)), scaled(GT[:]))
                dve.wait_ge(S_["g2"], n + 1)
                own.link(V.tensor_scalar(G2[:], G2[:], 0.044715, 1.0, ALU.mult, ALU.add))
                V.tensor_tensor(G2[:], G2[:], GT[:], ALU.mult).then_inc(S_["gelu_arg"], 1)
                s, c = units.use(*gates)
                dve.wait_ge(S_["gate_tanh"], 2 * n + 2)
                dve.sem_inc(S_[f"taken{s}"], 1)
                V.scalar_tensor_tensor(IT[:], IT[:], 1.0, XC[:], ALU.add, ALU.mult).then_inc(S_["gate_i_taken"], 1)
                dve.wait_ge(S_["gate_i_taken"], n + 2)
                if not last:
                    conv1(n + 1, ("rnn", n, 1))
                dve.wait_ge(S_["gelu_tanh"], n + 1)
                own.mark(V.scalar_tensor_tensor(GT[:], G2[:], 1.0, GT[:], ALU.add, ALU.mult))
                dve.wait_ge(S_["root"], n + 1)
                own.link(V.scalar_tensor_tensor(MT[:], AT[:], 1.0, MT[:], ALU.add, ALU.mult))
                own.link(V.scalar_tensor_tensor(MT[:], MT[:], 0.5, IT[:], ALU.mult, ALU.mult))
                own.link(V.tensor_tensor_scan(HS[:], AT[:], MT[:], 0.0, ALU.mult, ALU.add))
                V.scalar_tensor_tensor(HS[:], HS[:], 0.5, GT[:], ALU.mult, ALU.mult).then_inc(S_["ro_raw"], 1)
                dve.wait_ge(S_["ro_raw"], n + 1)
                dve.wait_ge(S_["ro_hi"], n + 1)
                V.tensor_tensor(RO[1][:, bass.ds(n, 1), :], HS[:].unsqueeze(1),
                                RO[0][:, bass.ds(n, 1), :].bitcast(F32), ALU.subtract).then_inc(S_["ro_lo"], 1)

            dve.sem_inc(S_["gate_i_taken"], 1)
            dve.wait_ge(S_["a_qk_lo"], 16)
            own.link(V.memset(XR[:, 0:3], 0.0))
            conv1(0, ("xr0", 0, 0))
            with dve.Fori(0, DC - 1) as n:
                own.enter(n, 8)
                rnn(n, False)
                own.leave(DC - 1)
            rnn(DC - 1, True)

            dve.wait_ge(S_["ro_lo"], DC)
            with dve.Fori(0, DC) as e:
                take("merge1", e, 1, scaled(GA[:, 0, :]))
                take("merge1", e, 2, scaled(GA[:, 1, :]))
                for j in range(2):
                    dve.wait_ge(S_["sg"], 2 * e + j + 1)
                    take("merge1", e, 3 * j, lambda bank: V.tensor_tensor(SG[:, j, :], bank[:], SG[:, j, :], ALU.mult))
                for j in range(2):
                    s, c = units.use("merge1", e, 3 * j)
                    dve.wait_ge(S_[f"taken{s}"], c)
                V.tensor_tensor(MG[:, bass.ds(e, 1), :], SG[:, 0:1, :], SG[:, 1:2, :], ALU.add).then_inc(S_["mg"], 1)
            for e in range(DC):
                dve.wait_ge(S_["mg_hi"], e + 1)
                V.tensor_tensor(AO[1][:, e, :], MG[:, e, :], AO[0][:, e, :].bitcast(F32), ALU.subtract
                                ).then_inc(S_["mg_lo"], 1)

            def add_to_x(name, it, j, e):
                x_e = X[:, bass.ds(e, 1), :]
                take(name, it, j, lambda bank: V.tensor_tensor(x_e, x_e, bank[:].unsqueeze(1), ALU.add))

            V.memset(ACC1[:], 0.0).then_inc(norm_event("n2", "acc", 0)[0], 1)
            for i in range(2):
                for j in range(4):
                    add_to_x("out1", i, j, 4 * i + j)
                    s, c = units.use("out1", i, j)
                    dve.wait_ge(S_[f"taken{s}"], c)
                    norm_chunk("n2", 4 * i + j, j % 2)
            norm_rstd("n2")

            def mlp_group(g, last=False):
                def lo(j):
                    dve.wait_ge(S_["u_hi"], 8 * g + j + 1)
                    V.tensor_tensor(UL[:, j, :], SU[:, j % 2, :], UH[:, j, :].bitcast(F32), ALU.subtract
                                    ).then_inc(S_["u_lo"], 1)

                for j in range(8):
                    take("mlp", g, j, lambda bank: V.scalar_tensor_tensor(TU[:, j % 2, :], bank[:], 0.0, RSTD[:],
                                                                          ALU.max, ALU.mult))
                    if j:
                        lo(j - 1)
                lo(7)
                if not last:
                    for j in range(8):
                        add_to_x("mlp", g, 8 + j, j)

            mlp_group(0)
            with dve.Fori(1, 3) as g:
                mlp_group(g)
            mlp_group(3, True)

            def norm_begin(tag, before):
                dve.wait_ge(*norm_event(before, "stat", 1))
                V.memset(ACC1[:], 0.0).then_inc(norm_event(tag, "acc", 0)[0], 1)

            def norm_chunks(tag, name, it, first, after=None):
                for e in range(DC):
                    wide = len(units.slots[name])
                    i, j = it + (first + e) // wide, (first + e) % wide
                    add_to_x(name, i, j, e)
                    s, c = units.use(name, i, j)
                    dve.wait_ge(S_[f"taken{s}"], c)
                    norm_chunk(tag, e, e % 2)
                    if after:
                        after(e)

            norm_begin("n3", "n2")
            norm_chunks("n3", "mlp", 3, 8)
            for part in (FONE[:], PLACE0[:], M2["VR"][:]):
                own.mark(V.memset(part, 1.0 if part.shape[0] == HEADS and part.shape[1] == S else 0.0))
            own.wait()
            own.link(V.tensor_copy(PLACE0[:, 96:104], ident[0:8, 0:8]))
            for k in ("VH", "VL"):
                for part in range(2):
                    ins = V.tensor_copy(M2[k][:, part], M2["VR"][:].rearrange("p (j e) -> p j e", j=NB))
                    if k == "VL" and part:
                        ins.then_inc(once("values_cleared")[0], 1)
                    else:
                        own.link(ins)
            V.tensor_copy(PLACE[:], PLACE0[:]).then_inc(once("place_made")[0], 1)
            dve.wait_ge(*once("above_made"))
            own.link(V.tensor_copy(ABOVER[:], above[:]))
            norm_rstd("n3")

            take("fgate", 0, 0, lambda bank: V.tensor_tensor(FG[:], bank[0:8, :], RSTD[0:8, :], ALU.mult))
            s, c = units.use("fgate", 0, 0)
            dve.wait_ge(S_[f"taken{s}"], c)
            own.link(V.tensor_scalar(FG[:], FG[:], small[0:8, FBIAS:FBIAS + 1], None, ALU.add))
            V.scalar_tensor_tensor(FA[:], FG[:], -1.0, FG[:], ALU.mult, ALU.max).then_inc(once("forget_abs")[0], 1)
            dve.wait_ge(*once("forget_exp"))
            V.tensor_scalar(FU[:], FE[:], 1.0, None, ALU.add).then_inc(once("forget_one_plus")[0], 1)
            own.mark(V.tensor_scalar(FT[:], FE[:], -0.5, 1.0, ALU.mult, ALU.add))
            dve.wait_ge(*once("forget_one_plus"))
            own.link(V.tensor_scalar(FA[:], FU[:], -1.0, 1e-30, ALU.add, ALU.max))
            own.mark(V.tensor_tensor(FT[:], FT[:], FE[:], ALU.mult))
            own.link(V.reciprocal(FA[:], FA[:]))
            own.link(V.tensor_tensor(FA[:], FA[:], FE[:], ALU.mult))
            dve.wait_ge(*once("forget_ln"))
            own.link(V.tensor_tensor(FA[:], FA[:], FLN[:], ALU.mult))
            own.link(V.tensor_tensor(FA[:], FA[:], FT[:], ALU.max))
            own.link(V.scalar_tensor_tensor(FG[:], FG[:], 0.0, FA[:], ALU.min, ALU.subtract))
            V.tensor_tensor_scan(FT[:], FONE[:], FG[:], 0.0, ALU.mult, ALU.add).then_inc(once("forget_cum")[0], 1)
            dve.wait_ge(*once("forget_cum"))
            dve.wait_ge(*once("forget_cum_hi"))
            V.tensor_tensor(FCL[:], FT[:], FCH[:].bitcast(F32), ALU.subtract).then_inc(once("forget_cum_lo")[0], 1)

            def take_q2(name, h, j):
                take(name, h, j, lambda bank: V.scalar_tensor_tensor(M2["QN"][:, 0, :], bank[:], 64 ** -0.5, RSTD[:],
                                                                     ALU.mult, ALU.mult))

            def v_lo2(tag):
                for part in range(2):
                    cols = slice(64 * part, 64 * part + 64)
                    V.tensor_tensor(M2["VL"][:, part, :, cols], OUTB[:].rearrange("p (j e) -> p j e", j=NB)[:, :, cols],
                                    M2["VH"][:, part, :, cols].bitcast(F32), ALU.subtract
                                    ).then_inc(S_[tag + "_v_lo"], 1)

            def lo2(tag, side, n):
                dve.wait_ge(S_[tag + "_qk_hi"], n)
                V.tensor_tensor(M2["QL"][:, side, :], M2["QN"][:, side, :], M2["QH"][:, side, :].bitcast(F32),
                                ALU.subtract).then_inc(S_[tag + "_qk_lo"], 1)

            def out_lo2(tag, Y, h, first=0):
                dve.wait_ge(S_[tag + "_o_hi"], first + h + 1)
                V.tensor_tensor(Y[1][:, bass.ds(h, 1), :], OUTB[:].unsqueeze(1),
                                Y[0][:, bass.ds(h, 1), :].bitcast(F32), ALU.subtract
                                ).then_inc(S_[tag + "_out_taken"], 1)

            def row_max2(t, part, bank):
                return V.tensor_reduce(NMAX[:, t:t + 1], bank, AX.X, ALU.max, negate=True)

            def scale_probs(M, kind, i, sums):
                own.link(V.reciprocal(RS[:, 2 * i:2 * i + 2], sums))
                at, wide = kind.offset(i), (i + 1 - kind.first(i)) * P
                for part in range(2):
                    p = M["PR"][:, part, at:at + wide]
                    ins = V.tensor_scalar(p, p, RS[:, 2 * i + part:2 * i + part + 1], None, ALU.mult)
                    if part == 0:
                        own.link(ins)
                return ins

            def decay_rows(h):
                for part in range(2):
                    V.tensor_scalar(FROW[:, part, :], FRIGHT[:], IND[:, bass.ds(2 * h + part, 1)], None, ALU.mult
                                    ).then_inc(S_["f_row"], 1)

            dve.wait_ge(*once("values_cleared"))
            take_q2("fox", 0, 0)
            take("fox", 0, 1, scaled(M2["QN"][:, 1, :]))
            dve.wait_ge(*once("forget_placed"))
            own.mark(V.tensor_scalar(FLEFT[:], WORK[0][:], SIDE[:, 1:2], None, ALU.add))
            own.link(V.tensor_scalar(FRIGHT[:], WORK[1][:], SIDE[:, 0:1], None, ALU.add))
            decay_rows(0)
            take("fox", 0, 2, scaled(M2["VR"][:]))
            for side in range(2):
                lo2("f", side, 1 + side)

            def fox(h, last):
                following = ("swa_first", 0) if last else ("fox", h + 1)
                softmax("f", M2, KIND_FOX, h, row_max2, lambda: v_lo2("f"),
                        lambda i: scale_probs(M2, KIND_FOX, i, SUM[:, 2 * i:2 * i + 2]),
                        lambda i: take_q2(*following, 0) if i == 2 else None)
                if not last:
                    decay_rows(h + 1)
                take(*following, 1, scaled(M2["QN"][:, 1, :]))
                for n in range(8):
                    probs_lo("f", M2, KIND_FOX, h, n)
                    if n in (2, 4):
                        lo2("f", n // 2 - 1, 2 * h + 2 + n // 2)
                out_lo2("f", YF, h)
                take(*following, 2, scaled(M2["VR"][:]))

            with dve.Fori(0, 3) as h:
                own.enter(h, 8)
                fox(h, False)
                own.leave(3)
            fox(3, True)

            dve.wait_ge(S_["f_v_hi"], 10)
            v_lo2("f")

            own.link(V.memset(ZP[:, 0:2], 0.0))

            def conv_unit(h, last, j):
                return ("swa_last", 0, j) if last else ("swa", h, 1 + j)

            def conv2(h, last, n):
                if n == 0:
                    take(*conv_unit(h, last, 0), scaled(CB))
                if n == 1:
                    take(*conv_unit(h, last, 1), scaled(CC))
                if n == 3:
                    take(*conv_unit(h, last, 2), scaled(ZP[:, 2:]))
                if n == 4:
                    for j in (0, 1, 2):
                        s, c = units.use(*conv_unit(h, last, j))
                        dve.wait_ge(S_[f"taken{s}"], c)
                    own.link(V.tensor_tensor(ZP[:, 2:], ZP[:, 2:], CC, ALU.mult))
                    own.link(V.tensor_scalar(CV, ZP[:, 0:S], par("conv_w_2", h), None, ALU.mult))
                if n in (5, 6):
                    own.link(V.scalar_tensor_tensor(CV, ZP[:, n - 4:n - 4 + S], par("conv_w_2", h + 4 * (n - 4)), CV,
                                                    ALU.mult, ALU.add))
                if n == 7:
                    V.tensor_tensor(CV, CV, CB, ALU.mult).then_inc(S_["yc_raw"], 1)

            def conv2_lo(h):
                dve.wait_ge(S_["yc_raw"], h + 1)
                dve.wait_ge(S_["yc_hi"], h + 1)
                V.tensor_tensor(YC[1][:, bass.ds(h, 1), :], CV.unsqueeze(1),
                                YC[0][:, bass.ds(h, 1), :].bitcast(F32), ALU.subtract).then_inc(S_["yc_lo"], 1)

            def swa(h, last):
                def row_max_sink(t, part, bank):
                    own.link(V.tensor_reduce(NMAX[:, t:t + 1], bank, AX.X, ALU.max, negate=True))
                    return V.tensor_tensor(NMAX[:, t:t + 1], NMAX[:, t:t + 1],
                                           small[:, bass.ds(NSINK + 4 * part + h, 1)], ALU.min)

                def normalise(i):
                    dve.wait_ge(S_["s_sink"], 8 * h + 2 * i + 2)
                    two = SUM[:, 2 * i:2 * i + 2]
                    own.link(V.tensor_tensor(two, two, SEXP[:, 2 * i:2 * i + 2], ALU.add))
                    return scale_probs(M2, KIND_SWA, i, two)

                softmax("f", M2, KIND_SWA, h + 4, row_max_sink, None, normalise)
                if not last:
                    take_q2("swa", h, 0)
                for n in range(8):
                    probs_lo("f", M2, KIND_SWA, h + 4, n)
                    conv2(h, last, n)
                    if n == 2 and not last:
                        lo2("f", 0, h + 11)
                conv2_lo(h)
                out_lo2("f", YS, h, 4)

            with dve.Fori(0, 3) as h:
                own.enter(h, 24)
                swa(h, False)
                own.leave(3)
            swa(3, True)

            dve.wait_ge(S_["f_out_taken"], 9)
            with dve.Fori(0, DC) as e:
                own.enter(e, 1)
                for j in range(3):
                    take("merge2", e, 1 + j, scaled(GA2[:, j, :]))
                dve.wait_ge(S_["sg2"], 3 * e + 2)
                take("merge2", e, 0, lambda bank: V.tensor_tensor(SG2[:, 0, :], bank[:], SG2[:, 0, :], ALU.mult))
                V.tensor_tensor(SG2[:, 1, :], WORK[0][:], SG2[:, 1, :], ALU.mult).then_inc(S_["m2_fox_taken"], 1)
                dve.wait_ge(S_["sg2"], 3 * e + 3)
                take("merge2", e, 4, lambda bank: V.tensor_tensor(SG2[:, 2, :], bank[:], SG2[:, 2, :], ALU.mult))
                s, c = units.use("merge2", e, 0)
                dve.wait_ge(S_[f"taken{s}"], c)
                dve.wait_ge(S_["m2_fox_taken"], e + 2)
                own.link(V.tensor_tensor(MX[:, 1, :], SG2[:, 0, :], SG2[:, 1, :], ALU.add))
                s, c = units.use("merge2", e, 4)
                dve.wait_ge(S_[f"taken{s}"], c)
                V.tensor_tensor(MX[:, 0, :], MX[:, 1, :], SG2[:, 2, :], ALU.add).then_inc(S_["mgc_raw"], 1)
                dve.wait_ge(S_["mgc_raw"], e + 1)
                dve.wait_ge(S_["mgc_hi"], e + 1)
                V.tensor_tensor(MGC[1][:, bass.ds(e, 1), :], MX[:, 0:1, :],
                                MGC[0][:, bass.ds(e, 1), :].bitcast(F32), ALU.subtract).then_inc(S_["mgc_lo"], 1)
                own.leave(DC)

            norm_begin("n4", "n3")
            V.memset(ACCM[:], 0.0).then_inc(S_["mem_acc"], 1)

            def mem_chunks(e):
                for m in mem_after(e):
                    dve.wait_ge(S_["mem_hi"], m + 1)
                    dve.wait_ge(S_["mem_sq"], m + 1)
                    V.scalar_tensor_tensor(MEMC[1][:, m, :], WORK[m % 2][:, 0:MEM], par("mem_norm_g_2", m),
                                           MEMC[0][:, m, :].bitcast(F32), ALU.mult, ALU.subtract
                                           ).then_inc(S_["mem_lo"], 1)
                    dve.wait_ge(S_["mem_acc"], m + 1)
                    V.tensor_tensor(ACCM[:], ACCM[:], SQM[:, m % 2, :], ALU.add).then_inc(S_["mem_acc"], 1)

            norm_chunks("n4", "out2", 0, 0, mem_chunks)
            norm_rstd("n4")
            dve.wait_ge(*once("mem_std"))
            own.link(V.reciprocal(RSTDM[:], STDM[:]))

            def cross_take(h, kinds):
                for kind in kinds:
                    for j in range(2):
                        if kind == "q":
                            take("cross", h, j, lambda bank: V.scalar_tensor_tensor(
                                XQ[:, j, :], bank[:], 256 ** -0.5, RSTD[:], ALU.mult, ALU.mult))
                        else:
                            unit, dst = (2 + j, XK) if kind == "k" else (4 + j, XV)
                            take("cross", h, unit, lambda bank: V.tensor_tensor(
                                dst[:, j, :], bank[:, 0:MEM], RSTDM[:], ALU.mult))

            def cross_lo(h):
                for j in range(2):
                    dve.wait_ge(S_["x_q_hi"], 2 * h + j + 1)
                    V.tensor_tensor(XQC[1][:, j, :], XQ[:, j, :], XQC[0][:, j, :].bitcast(F32), ALU.subtract
                                    ).then_inc(S_["x_q_lo"], 1)
                dve.wait_ge(S_["x_k_hi"], h + 1)
                V.tensor_tensor(XKC[1][:], XK[:], XKC[0][:].bitcast(F32), ALU.subtract).then_inc(S_["x_k_lo"], 1)

            cross_take(0, "qkv")
            cross_lo(0)

            def cross(h, last):
                dve.wait_ge(S_["x_v_hi"], h + 1)
                V.tensor_tensor(XVC[1][:], OUTB[:].rearrange("p (m e) -> p m e", m=2), XVC[0][:].bitcast(F32),
                                ALU.subtract).then_inc(S_["x_v_lo"], 1)
                for i in range(NB):
                    dve.wait_ge(S_["x_score"], 4 * h + i + 1)
                    V.tensor_reduce(NMAX[:, i:i + 1], WORK[i % 2][:, 0:MEM], AX.X, ALU.max, negate=True
                                    ).then_inc(S_["x_row_max"], 1)
                    if i:
                        x_normalise(h, i - 1)
                x_normalise(h, NB - 1)
                if not last:
                    cross_take(h + 1, "q")
                for mb in range(2):
                    dve.wait_ge(S_["x_pt_hi"], 2 * h + mb + 1)
                    V.tensor_tensor(XTC[1][:, mb, :], WORK[mb][:], XTC[0][:, mb, :].bitcast(F32), ALU.subtract
                                    ).then_inc(S_["x_pt_lo"], 1)
                if not last:
                    cross_take(h + 1, "k")
                    cross_lo(h + 1)
                for c, bank in enumerate((OUTB, STAT)):
                    dve.wait_ge(S_["x_out_hi"], 2 * h + c + 3)
                    V.tensor_tensor(XO[1][:, bass.ds(2 * h + c, 1), :], bank[:].unsqueeze(1),
                                    XO[0][:, bass.ds(2 * h + c, 1), :].bitcast(F32), ALU.subtract
                                    ).then_inc(S_["x_out_lo"], 1)
                if not last:
                    cross_take(h + 1, "v")

            def x_normalise(h, i):
                dve.wait_ge(S_["x_exp"], 4 * h + i + 1)
                own.link(V.reciprocal(RS[:, i:i + 1], SUM[:, i:i + 1]))
                V.tensor_scalar(XPR[:, i, :], XPR[:, i, :], RS[:, i:i + 1], None, ALU.mult
                                ).then_inc(S_["x_probs"], 1)

            with dve.Fori(0, 3) as h:
                own.enter(h, 4)
                cross(h, False)
                own.leave(3)
            cross(3, True)
            norm_begin("n5", "n4")
            norm_chunks("n5", "xout", 0, 0)
            norm_rstd("n5")

            def ffn_group(name, g, last):
                wide = len(units.slots[name]) // 2 - 4
                base = 16 if name == "ffn_tail" else 8 * g

                def lo(j):
                    dve.wait_ge(S_["ff_hi"], base + j + 1)
                    V.tensor_tensor(FF[1][:, j, :], FUP[:, j % 2, :], FF[0][:, j, :].bitcast(F32), ALU.subtract
                                    ).then_inc(S_["ff_lo"], 1)

                for j in range(wide):
                    take(name, g, 2 * j, scaled(FGA[:, j % 2, :]))
                    if j:
                        lo(j - 1)
                    take(name, g, 2 * j + 1, scaled(FUP[:, j % 2, :]))
                    s, c = units.use(name, g, 2 * j + 1)
                    dve.wait_ge(S_[f"taken{s}"], c)
                    dve.wait_ge(S_["ff_silu"], base + j + 1)
                    V.tensor_tensor(FUP[:, j % 2, :], FUP[:, j % 2, :], FGA[:, j % 2, :], ALU.mult
                                    ).then_inc(S_["ff_raw"], 1)
                    dve.wait_ge(S_["ff_raw"], base + j + 1)
                lo(wide - 1)
                if not last:
                    for j in range(DC):
                        add_to_x(name, g, 2 * wide + j, j)

            ffn_group("ffn", 0, False)
            ffn_group("ffn", 1, False)
            ffn_group("ffn_tail", 0, True)
            norm_begin("n6", "n5")
            def out_of_bank(e):
                dve.wait_ge(S_["y_t"], e + 1)
                V.tensor_copy(YTOK[:, :, e * P:(e + 1) * P], WORK[e % 2][:].rearrange("p (t f) -> p t f", t=NB)
                              ).then_inc(S_["y_taken"], 1)

            for e in range(DC):
                add_to_x("ffn_tail", 0, 12 + e, e)
                dve.wait_ge(*norm_event("n6", "sq", e + 1))
                dve.wait_ge(*norm_event("n6", "acc", e + 1))
                V.tensor_tensor(ACC1[:], ACC1[:], SQ1[:, e % 2, :], ALU.add).then_inc(norm_event("n6", "acc", 0)[0], 1)
                if e >= 2:
                    out_of_bank(e - 2)

            out_of_bank(DC - 2)
            out_of_bank(DC - 1)
            dve.wait_ge(*norm_event("n6", "std", 1))
            V.reciprocal(NMAX[:, 0:NB], RS[:, 0:NB]).then_inc(S_["y_rstd"], 1)
            dve.wait_ge(S_["y_rstd"], 1)
            dve.wait_ge(S_["y_taken"], DC)
            for t in range(0, NB, 2):
                V.tensor_scalar(YTOK[:, t, :], YTOK[:, t, :], NMAX[:, t:t + 1], None, ALU.mult
                                ).then_inc(S_["y_scaled_v"], 1)


_VECTORS = {"conv_b", "b_rg_a", "b_rg_x"}


def kernel(**inputs):
    import concourse.bacc as bacc
    from concourse.bass_utils import run_bass_kernel_spmd as run

    nc = bacc.Bacc("TRN2", target_bir_lowering=False, num_devices=1)
    arrays, w = {}, {}

    def give(name, a):
        a = np.ascontiguousarray(a)
        arrays[f"in_{name}"] = a
        return nc.dram_tensor(f"in_{name}", a.shape, mybir.dt.from_np(a.dtype), kind="ExternalInput").ap()

    matrices = {"w_in", "w_rg_a", "w_rg_x", "w_proj_attn", "w_proj_rnn", "w_out", "w_up", "w_down", "rel_bias",
                "w_in_2", "w_branch_2", "w_mix_out_2", "rel_bias_2", "w_xq_2", "w_xkv_2", "w_xo_2",
                "w_ffn_gate_2", "w_ffn_up_2", "w_ffn_down_2", "mem_2", "x"}
    for name in inputs:
        a = np.asarray(inputs[name])
        w[name] = give(name, a.reshape(-1, a.shape[-1]) if name in matrices else a.reshape(-1))
    causal, window = bucket_rows()
    rows = give("causal_buckets", causal), give("window_buckets", window)
    out = nc.dram_tensor("out_0", (1, S, D), F32, kind="ExternalOutput").ap()
    program(nc, w["x"], out.rearrange("a s d -> (a s) d"), w, *rows)
    r = run(nc, [arrays], core_ids=[0])
    return r.results[0]["out_0"]
```
